# Optimizing a Trainium2 kernel written in Bass

```python
import math
import jax, jax.numpy as jnp
from jax import lax
import numpy as np

D_MODEL = 2048
BATCH = 1
SEQ = 256
DEPTH = 1

MIX_WIDTH = D_MODEL
DIFF_WIDTH = MIX_WIDTH // 2
SB_WIDTH = MIX_WIDTH - DIFF_WIDTH
DIFF_HEADS = 4
DIFF_QK_DIM = DIFF_WIDTH // (2 * DIFF_HEADS)
DIFF_V_DIM = 2 * DIFF_QK_DIM
SB_HEADS = 8
SB_HEAD_DIM = SB_WIDTH // SB_HEADS
D_FF = ((8 * D_MODEL // 3 + 255) // 256) * 256
ROPE_THETA = 500000.0
ROPE_DIM = DIFF_QK_DIM // 4
Q_BLOCK = 128
EPS = 1e-5
DIFF_QK_COLS = DIFF_HEADS * DIFF_QK_DIM
DIFF_V_COLS = DIFF_HEADS * DIFF_V_DIM
IN_COLS = 4 * DIFF_QK_COLS + DIFF_V_COLS + 3 * SB_WIDTH

kernel_name = "hybrid_diffattn_stickbreaking_macaron"

def _rmsnorm(x, g):
    xf = x.astype(jnp.float32)
    y = xf * lax.rsqrt(jnp.mean(xf * xf, axis=-1, keepdims=True) + EPS)
    return (y * g.astype(jnp.float32)).astype(x.dtype)

def _swiglu(x, w_gate, w_up, w_down):
    return (jax.nn.silu(x @ w_gate) * (x @ w_up)) @ w_down

def _rope_tables(seq):
    pos = jnp.arange(seq, dtype=jnp.float32)
    inv_freq = ROPE_THETA ** (-jnp.arange(0, ROPE_DIM, 2, dtype=jnp.float32) / ROPE_DIM)
    ang = pos[:, None] * inv_freq[None, :]
    return jnp.cos(ang)[None, :, None, :], jnp.sin(ang)[None, :, None, :]

def _partial_rope(x, cos, sin):
    xf = x.astype(jnp.float32)
    half = ROPE_DIM // 2
    x1, x2, rest = xf[..., :half], xf[..., half:ROPE_DIM], xf[..., ROPE_DIM:]
    out = jnp.concatenate([x1 * cos - x2 * sin, x2 * cos + x1 * sin, rest], axis=-1)
    return out.astype(x.dtype)

def _softmax_map(q, k, mask, t0, t1):
    s = jnp.einsum('bqhd,bkhd->bhqk', q[:, t0:t1], k[:, :t1]).astype(jnp.float32) * (DIFF_QK_DIM ** -0.5)
    return jax.nn.softmax(jnp.where(mask, s, -jnp.inf), axis=-1)

def _diff_attention(q1, q2, k1, k2, v, lam):
    seq = q1.shape[1]
    vf = v.astype(jnp.float32)
    outs = []
    for i in range(seq // Q_BLOCK):
        t0, t1 = i * Q_BLOCK, (i + 1) * Q_BLOCK
        mask = jnp.arange(t0, t1)[:, None] >= jnp.arange(t1)[None, :]
        w = _softmax_map(q1, k1, mask, t0, t1) - lam * _softmax_map(q2, k2, mask, t0, t1)
        outs.append(jnp.einsum('bhqk,bkhd->bqhd', w, vf[:, :t1]))
    return jnp.concatenate(outs, axis=1)

def _stick_breaking(q, k, v):
    seq = q.shape[1]
    vf = v.astype(jnp.float32)
    scale = SB_HEAD_DIM ** -0.5
    outs = []
    for i in range(seq // Q_BLOCK):
        t0, t1 = i * Q_BLOCK, (i + 1) * Q_BLOCK
        mask = jnp.arange(t0, t1)[:, None] > jnp.arange(t1)[None, :]
        z = jnp.einsum('bqhd,bkhd->bhqk', q[:, t0:t1], k[:, :t1]).astype(jnp.float32) * scale
        log_1m_beta = jnp.where(mask, jax.nn.log_sigmoid(-z), 0.0)
        tail = lax.cumsum(log_1m_beta, axis=3, reverse=True) - log_1m_beta
        a = jnp.where(mask, jnp.exp(jax.nn.log_sigmoid(z) + tail), 0.0)
        outs.append(jnp.einsum('bhqk,bkhd->bqhd', a, vf[:, :t1]))
    return jnp.concatenate(outs, axis=1)

def setup_inputs(seed: int = 0) -> dict:
    key = jax.random.key(seed)
    ks = jax.random.split(key, 24)
    f32 = jnp.float32
    nrm = lambda k, shape, s: jax.random.normal(k, shape, f32) * s
    gain = lambda k, n: 1.0 + 0.01 * jax.random.normal(k, (DEPTH, n), f32)
    return {
        "x": jax.random.normal(ks[0], (BATCH, SEQ, D_MODEL), f32),
        "ffn1_norm": gain(ks[1], D_MODEL),
        "ffn1_w_gate": nrm(ks[2], (DEPTH, D_MODEL, D_FF), D_MODEL ** -0.5),
        "ffn1_w_up": nrm(ks[3], (DEPTH, D_MODEL, D_FF), D_MODEL ** -0.5),
        "ffn1_w_down": nrm(ks[4], (DEPTH, D_FF, D_MODEL), D_FF ** -0.5),
        "mix_norm": gain(ks[5], D_MODEL),
        "w_in": nrm(ks[6], (DEPTH, D_MODEL, IN_COLS), D_MODEL ** -0.5),
        "q_norm": gain(ks[7], DIFF_QK_DIM),
        "k_norm": gain(ks[8], DIFF_QK_DIM),
        "lambda_q1": nrm(ks[9], (DEPTH, DIFF_QK_DIM), 0.1),
        "lambda_k1": nrm(ks[10], (DEPTH, DIFF_QK_DIM), 0.1),
        "lambda_q2": nrm(ks[11], (DEPTH, DIFF_QK_DIM), 0.1),
        "lambda_k2": nrm(ks[12], (DEPTH, DIFF_QK_DIM), 0.1),
        "subln": gain(ks[13], DIFF_V_DIM),
        "w_out": nrm(ks[14], (DEPTH, MIX_WIDTH, D_MODEL), MIX_WIDTH ** -0.5),
        "ffn2_norm": gain(ks[15], D_MODEL),
        "ffn2_w_gate": nrm(ks[16], (DEPTH, D_MODEL, D_FF), D_MODEL ** -0.5),
        "ffn2_w_up": nrm(ks[17], (DEPTH, D_MODEL, D_FF), D_MODEL ** -0.5),
        "ffn2_w_down": nrm(ks[18], (DEPTH, D_FF, D_MODEL), D_FF ** -0.5),
        "final_norm": gain(ks[19], D_MODEL),
    }

def reference(x, ffn1_norm, ffn1_w_gate, ffn1_w_up, ffn1_w_down, mix_norm, w_in, q_norm, k_norm,
              lambda_q1, lambda_k1, lambda_q2, lambda_k2, subln, w_out,
              ffn2_norm, ffn2_w_gate, ffn2_w_up, ffn2_w_down, final_norm):
    b, s, _ = x.shape
    cos, sin = _rope_tables(s)
    for l in range(DEPTH):
        x = x + 0.5 * _swiglu(_rmsnorm(x, ffn1_norm[l]), ffn1_w_gate[l], ffn1_w_up[l], ffn1_w_down[l])

        u = _rmsnorm(x, mix_norm[l]) @ w_in[l]
        c = np.cumsum([0, DIFF_QK_COLS, DIFF_QK_COLS, DIFF_QK_COLS, DIFF_QK_COLS,
                       DIFF_V_COLS, SB_WIDTH, SB_WIDTH, SB_WIDTH]).tolist()
        q1, q2, k1, k2, dv, sq, sk, sv = [u[..., c[i]:c[i + 1]] for i in range(8)]

        def prep(t, g):
            t = t.reshape(b, s, DIFF_HEADS, DIFF_QK_DIM)
            return _partial_rope(_rmsnorm(t, g), cos, sin)
        q1, q2 = prep(q1, q_norm[l]), prep(q2, q_norm[l])
        k1, k2 = prep(k1, k_norm[l]), prep(k2, k_norm[l])
        dv = dv.reshape(b, s, DIFF_HEADS, DIFF_V_DIM)
        lambda_init = 0.8 - 0.6 * math.exp(-0.3 * l)
        lam = (jnp.exp(jnp.sum(lambda_q1[l].astype(jnp.float32) * lambda_k1[l].astype(jnp.float32)))
               - jnp.exp(jnp.sum(lambda_q2[l].astype(jnp.float32) * lambda_k2[l].astype(jnp.float32)))
               + lambda_init)
        a_out = _diff_attention(q1, q2, k1, k2, dv, lam)
        a_out = _rmsnorm(a_out, subln[l]) * (1.0 - lambda_init)
        a_out = a_out.reshape(b, s, DIFF_WIDTH).astype(x.dtype)

        sq = sq.reshape(b, s, SB_HEADS, SB_HEAD_DIM)
        sk = sk.reshape(b, s, SB_HEADS, SB_HEAD_DIM)
        sv = sv.reshape(b, s, SB_HEADS, SB_HEAD_DIM)
        b_out = _stick_breaking(sq, sk, sv).reshape(b, s, SB_WIDTH).astype(x.dtype)

        x = x + jnp.concatenate([a_out, b_out], axis=-1) @ w_out[l]

        x = x + 0.5 * _swiglu(_rmsnorm(x, ffn2_norm[l]), ffn2_w_gate[l], ffn2_w_up[l], ffn2_w_down[l])

        x = _rmsnorm(x, final_norm[l])
    return x


_drawn_inputs = setup_inputs


def setup_inputs(seed=0):
    import zlib

    import numpy as np

    out = dict(_drawn_inputs(seed))
    spreads = {}
    factors = {'ffn1_norm': 8.0,
     'mix_norm': 5.838,
     'q_norm': 23.653,
     'k_norm': 23.969,
     'lambda_q1': 3.513,
     'subln': 64.0,
     'ffn2_norm': 44.51,
     'final_norm': 33.894,
     'lambda_q2': 6.841,
     'lambda_k2': 3.734}
    for name, (base, spread) in spreads.items():
        noise = np.random.default_rng([zlib.crc32(name.encode()), seed]).standard_normal(out[name].shape)
        drawn = base * np.exp(spread * noise) if base else spread * noise
        out[name] = __import__('jax').numpy.asarray(drawn.astype(out[name].dtype))
    for name, factor in factors.items():
        out[name] = (out[name] * factor).astype(out[name].dtype)
    return out
```

```python
from contextlib import ExitStack

import concourse.bass as bass
from concourse import mybir

F32 = mybir.dt.float32
F32R = mybir.dt.float32r
ALU = mybir.AluOpType
ACT = mybir.ActivationFunctionType
AX_X = mybir.AxisListType.X

P = 128
STRIP = 256
EPS = 1e-5
LAMBDA_INIT = 0.2
NEG = -1e30
RAW_SLOTS = 4
SPLIT_SLOTS = 2
K_SLOT = 8

CONST_COLS = {"ones": 128, "ident": 128, "tri": 128, "causal": 384, "strict": 128, "strict_neg": 128,
              "cos": 256, "sin": 256, "rot": 32, "minus_half": 1}
PARAM_COLS = {"gain": 64, "q_norm": 1, "k_norm": 1, "subln": 2, "lambda": 4}
NORM_MIX, NORM_FFN2, NORM_FINAL = 1, 2, 3


def columns(table):
    at, out = 0, {}
    for name, n in table.items():
        out[name] = (at, at + n)
        at += n
    return out, at


def hybrid_layer(nc, x_t, params, consts, ffn1_gate, ffn1_up, ffn1_down, w_in, w_out,
                 ffn2_gate, ffn2_up, ffn2_down, out_t):
    D = w_out.shape[1]
    FF = ffn1_gate.shape[1]
    T = x_t.shape[2]
    KB = D // P
    NS = D // STRIP
    HALF_K = KB // 2
    assert T == 256 and KB == 16 and FF % (2 * STRIP) == 0
    SCALE = float(P) ** -0.5

    phases = []
    s = g = r = 0
    ff_parts = []
    at = 0
    for n in (8, 8, FF // STRIP - 16):
        ff_parts.append((at, n))
        at += n
    def plan_ffn(gate, up, down, norm_in, norm_out):
        nonlocal s, g, r
        for part, (f0, n) in enumerate(ff_parts):
            phases.append({"kind": "ffn_in", "s0": s, "g0": g, "bodies": n, "kn": HALF_K, "f0": f0,
                           "gate": gate, "up": up, "norm": norm_in, "entry": part == 0})
            s, g = s + 2 * n, g + n
            last = part == len(ff_parts) - 1
            phases.append({"kind": "residual", "s0": s, "r0": r, "bodies": NS // 2, "kn": n, "k0": 2 * f0,
                           "w": down, "g0": g - n, "factor": 0.5, "norm": norm_out if last else None})
            s, r = s + NS, r + NS
    plan_ffn(ffn1_gate, ffn1_up, ffn1_down, 0, NORM_MIX)
    phases.append({"kind": "mix", "s0": s, "bodies": 12, "kn": HALF_K})
    s += 24
    phases.append({"kind": "residual", "s0": s, "r0": r, "bodies": NS // 2, "kn": HALF_K, "k0": 0,
                   "w": w_out, "g0": None, "factor": 1.0, "norm": NORM_FFN2})
    s, r = s + NS, r + NS
    plan_ffn(ffn2_gate, ffn2_up, ffn2_down, NORM_FFN2, NORM_FINAL)
    for n, ph in enumerate(phases):
        ph["next_kn"] = phases[n + 1]["kn"] if n + 1 < len(phases) else None

    QK = D // 4
    SBW = D // 2
    mix_strips = []
    for p in range(2):
        for t in range(4):
            mix_strips.append(("diff_qk", 4 * p + t, (t * QK) // STRIP + p))
        for h in range(2):
            mix_strips.append(("diff_v", 2 * p + h, (4 * QK) // STRIP + 2 * p + h))
    sb0 = (4 * QK + SBW) // STRIP
    sb = lambda kind, p: (("sb_v", 4 + p, sb0 + 2 * (SBW // STRIP) + p) if kind == "v" else
                          ("sb_qk", 2 * p + (kind == "k"), sb0 + (kind == "k") * (SBW // STRIP) + p))
    for kind, p in (("q", 0), ("k", 0), ("v", 0), ("q", 1), ("k", 1), ("v", 1),
                    ("q", 2), ("k", 2), ("q", 3), ("k", 3), ("v", 2), ("v", 3)):
        mix_strips.append(sb(kind, p))

    pe_steps = [(1, "norm", NORM_MIX), (2, "norm_spread", NORM_MIX), (3, "qk_norm", 0), (4, "qk_spread", 0)]
    for n, m in enumerate((1, 2, 3, 6, 7, 8, 9), start=1):
        pe_steps += [(2 * m + 2, "qk_norm", n), (2 * m + 3, "qk_spread", n)]
    for p in range(2):
        pe_steps += [(12 * p + 10, "scores", p), (12 * p + 15, "turn", p), (12 * p + 16, "values", p),
                     (12 * p + 17, "out_norm", p), (12 * p + 18, "out_spread", p)]
    for p, (a, b, c) in enumerate(((29, 31, 33), (34, 36, 38), (40, 42, 46), (44, 46, 48))):
        pe_steps += [(a, "sb_scores", p), (b, "sb_sums", p), (c, "sb_values", p)]
    rank = {"values": 0, "sb_values": 0, "qk_spread": 0, "out_spread": 0}
    pe_steps.sort(key=lambda e: (e[0], rank.get(e[1], 1)))
    banks = {"lambda": "X", "norm": "X", "norm_spread": "Y", "qk_norm": "X", "qk_spread": "Y", "scores": "XY",
             "turn": "X", "values": "Y", "out_norm": "X", "out_spread": "Y", "sb_scores": "X", "sb_sums": "Y", "sb_values": "X"}
    order = [("lambda", 0), ("norm", 0), ("norm_spread", 0)] + [e[1:] for e in pe_steps]
    order += [(kind, n) for n in (NORM_FFN2, NORM_FINAL) for kind in ("norm", "norm_spread")]
    before = {}
    for n, step in enumerate(order):
        before[step] = {next(e for e in reversed(order[:n]) if b in banks[e[0]])
                        for b in banks[step[0]] if any(b in banks[e[0]] for e in order[:n])}

    with ExitStack() as ctx:
        def sbuf(name, shape, dt=F32):
            return ctx.enter_context(nc.sbuf_tensor(name, [P, *shape], dt))

        def sem(name):
            return ctx.enter_context(nc.semaphore(name))

        x_res = sbuf("x_res", [NS, 2, T])
        x_split = sbuf("x_split", [NS, 2, 2, T], F32R)
        h_split = sbuf("h_split", [NS, 2, 2, T], F32R)
        w_raw = sbuf("w_raw", [RAW_SLOTS, K_SLOT * STRIP])
        w_split = sbuf("w_split", [SPLIT_SLOTS, 2, K_SLOT * STRIP], F32R)
        lo_sum = sbuf("lo_sum", [2, 2, T])
        strip_sum = sbuf("strip_sum", [2, 2, T])
        squares = sbuf("squares", [2, 2, T])
        silu_out = sbuf("silu_out", [2, T])
        square_sum = sbuf("square_sum", [2, T])
        mean_sq = sbuf("mean_sq", [4])
        diag = sbuf("diag", [4, P])
        rstd = sbuf("rstd", [T])
        rstd_tok = sbuf("rstd_tok", [2])
        const_at, const_n = columns(CONST_COLS)
        param_at, param_n = columns(PARAM_COLS)
        const_sb = sbuf("const_sb", [const_n])
        param_sb = sbuf("param_sb", [param_n])
        const = lambda name: const_sb[:, const_at[name][0]:const_at[name][1]]
        param = lambda name: param_sb[:, param_at[name][0]:param_at[name][1]]
        gain = param("gain").rearrange("p (n k) -> p n k", n=4)
        cos_gain = sbuf("cos_gain", [2, T])
        rot_gain = sbuf("rot_gain", [2, 32])
        subln_gain = sbuf("subln_gain", [2])
        lam_in = sbuf("lam_in", [2])
        lam_exp = sbuf("lam_exp", [2])
        lam_diff = sbuf("lam_diff", [1])
        neg_lam = sbuf("neg_lam", [1])
        warm = sbuf("warm", [1])
        qk = sbuf("qk", [4, 2, T])
        v = sbuf("v", [2, 2, STRIP])
        prob = sbuf("prob", [4, 384])
        prob_t = sbuf("prob_t", [2, 384])
        head_out = sbuf("head_out", [2, 2, T])
        roped = sbuf("roped", [2, T])
        rot_sin = sbuf("rot_sin", [2, T])
        head_mean = sbuf("head_mean", [4])
        head_rstd = sbuf("head_rstd", [4])
        seg_max = sbuf("seg_max", [4, 3])
        neg_max = sbuf("neg_max", [4, 2])
        exp_sum = sbuf("exp_sum", [4, 2])
        inv_sum = sbuf("inv_sum", [4, 3])
        out_sq = prob[:, 0:3, :].rearrange("p a b -> p (a b)")[:, 0:1024].rearrange("p (h d t) -> p h d t", h=2, d=2)
        z = prob[:, 0:2, :]
        softplus = prob[:, 2:4, :]
        sb_weight = prob_t[:, :, :]
        psum = ctx.enter_context(nc.psum_tensor("psum", [P, 8, 512], F32))

        landed = [sem(f"chunk_landed{n}") for n in range(RAW_SLOTS)]
        x_landed = [sem(f"x_landed{n}") for n in range(4)]
        params_landed = sem("params_landed")
        consts_landed = sem("consts_landed")
        out_written = sem("out_written")
        hi_made = sem("hi_made")
        lo_made = sem("lo_made")
        chunk_used = sem("chunk_used")
        lo_copied = sem("lo_copied")
        psum_freed = sem("psum_freed")
        scaled = sem("scaled")
        silu_done = sem("silu_done")
        hidden_done = sem("hidden_done")
        hidden_hi = sem("hidden_hi")
        hidden_ready = sem("hidden_ready")
        res_done = sem("res_done")
        squared = sem("squared")
        x_hi_made = sem("x_hi_made")
        x_ready = sem("x_ready")
        squares_added = sem("squares_added")
        norm_done = sem("norm_done")
        norm_mean = sem("norm_mean")
        norm_power = sem("norm_power")
        norm_diag = sem("norm_diag")
        norm_spread_done = sem("norm_spread_done")
        norm_ready = sem("norm_ready")
        prepared = sem("prepared")
        lam_ready = sem("lam_ready")
        out_ready = sem("out_ready")
        lam_ones = sem("lam_ones")
        lam_exped = sem("lam_exped")
        mix_scaled = sem("mix_scaled")
        v_ready = sem("v_ready")
        qk_squared = sem("qk_squared")
        qk_cosined = sem("qk_cosined")
        qk_normed = sem("qk_normed")
        qk_mean_done = sem("qk_mean_done")
        rot_done = sem("rot_done")
        qk_roped = sem("qk_roped")
        qk_power_done = sem("qk_power_done")
        qk_diag = sem("qk_diag")
        qk_spread_done = sem("qk_spread_done")
        qk_ready = sem("qk_ready")
        scores_done = sem("scores_done")
        scored = sem("scored")
        max_step = sem("max_step")
        exped = sem("exped")
        weight_step = sem("weight_step")
        turned = sem("turned")
        turn_copied = sem("turn_copied")
        values_done = sem("values_done")
        out_copied = sem("out_copied")
        out_squared = sem("out_squared")
        out_summed = sem("out_summed")
        out_mean = sem("out_mean")
        out_power_done = sem("out_power_done")
        out_diag = sem("out_diag")
        out_spread_done = sem("out_spread_done")
        out_normed = sem("out_normed")
        out_hi = sem("out_hi")
        diff_ready = sem("diff_ready")
        sb_scores_done = sem("sb_scores_done")
        sb_abs = sem("sb_abs")
        sb_z = sem("sb_z")
        sb_log = sem("sb_log")
        sb_soft = sem("sb_soft")
        sb_sums_done = sem("sb_sums_done")
        sb_expo = sem("sb_expo")
        sb_weights = sem("sb_weights")
        sb_values_done = sem("sb_values_done")
        sb_hi = sem("sb_hi")
        sb_ready = sem("sb_ready")

        LO_CREDIT = 2 * RAW_SLOTS
        USED_CREDIT = SPLIT_SLOTS
        FREED_CREDIT = 2

        hi_value = lambda c, half: 2 * c + half + 1
        lo_value = lambda c: LO_CREDIT + 2 * (c + 1)
        used_value = lambda c: USED_CREDIT + c + 1
        freed_value = lambda s: FREED_CREDIT + s + 1

        bank_freed = {
            "lambda": lambda n: (lam_exped, 1), "norm": lambda n: (norm_mean, n + 1),
            "norm_spread": lambda n: (norm_ready, n + 1), "qk_spread": lambda n: (qk_ready, n + 1),
            "out_spread": lambda n: (out_normed, n + 1),
            "qk_norm": lambda n: (rot_done, n + 1), "scores": lambda n: (scored, n + 1),
            "turn": lambda n: (turn_copied, n + 1), "values": lambda n: (out_squared, n + 1),
            "out_norm": lambda n: (out_mean, n + 1), "sb_scores": lambda n: (sb_z, n + 1),
            "sb_sums": lambda n: (sb_expo, 2 * n + 1), "sb_values": lambda n: (sb_ready, n + 1),
        }

        def loop(eng, n, body, first=False, last=False, unroll=1):
            a, b = int(first), n - int(last)
            if first:
                body(0)
            end = a + (b - a) // unroll * unroll
            if end > a:
                with eng.Fori(a, end, unroll) as i:
                    for u in range(unroll):
                        body(i + u if u else i)
            for i in range(end, b):
                body(i)
            if last and n > int(first):
                body(n - 1)

        def both(ap):
            return ap.unsqueeze(1).broadcast_to([ap.shape[0], 2, ap.shape[1]])

        def weights_of(ph):
            def rows(w, strip, k0, kn):
                return w.rearrange("(k p) (s n) -> p k s n", p=P, n=STRIP)[:, k0:k0 + kn, strip, :]
            if ph["kind"] == "ffn_in":
                return lambda i, j: rows(ph["gate"] if j < 2 else ph["up"], ph["f0"] + i, HALF_K * (j % 2), HALF_K)
            if ph["kind"] == "residual":
                return lambda i, j: rows(ph["w"], 2 * i + j // 2, ph["k0"] + ph["kn"] * (j % 2), ph["kn"])
            return lambda i, j: rows(w_in, mix_strips[2 * i + j // 2][2], HALF_K * (j % 2), HALF_K)

        block = ctx.enter_context(nc.Block())

        @block.sync
        def _(sp):
            for ph in phases:
                source = weights_of(ph)

                def four_chunks(i):
                    for j in range(4):
                        c = 2 * ph["s0"] + 4 * i + j
                        sp.wait_ge(lo_made, 2 * c + 2)
                        dst = w_raw[:, j, 0:ph["kn"] * STRIP].rearrange("p (k n) -> p k n", n=STRIP)
                        sp.dma_start(dst, source(i, j)).then_inc(landed[j], 16)

                if ph["kind"] == "mix":
                    for i in range(ph["bodies"]):
                        four_chunks(i)
                else:
                    loop(sp, ph["bodies"], four_chunks)
            for n in range(4):
                sp.wait_ge(out_ready, n + 1)
                sp.dma_start(out_t[:, 4 * n:4 * n + 4, :],
                             x_res[:, 2 * n:2 * n + 2, :, :].rearrange("p s k t -> p (s k) t")).then_inc(out_written, 16)
            sp.wait_ge(out_written, 64)

        @block.gpsimd
        def _(pool):
            pool.dma_start(param_sb[:, :], params).then_inc(params_landed, 16)
            pool.dma_start(const_sb[:, :], consts).then_inc(consts_landed, 16)
            pool.wait_ge(consts_landed, 16)

            def power(out, in_, done):
                nc.gpsimd.tensor_tensor(out, in_, const("minus_half").broadcast_to(out.shape), ALU.pow).then_inc(done, 1)

            def norm_rstd(n):
                pool.wait_ge(norm_mean, n + 1)
                power(rstd_tok[:, :], mean_sq[:, 0:2], norm_power)

            norm_rstd(0)
            norm_rstd(NORM_MIX)
            pool.wait_ge(prepared, 1)

            def rotary_cos(n):
                pool.wait_ge(mix_scaled, n + 1)
                if n:
                    pool.wait_ge(qk_ready, n)
                nc.gpsimd.tensor_tensor(roped[:, :, :], strip_sum[:, n % 2, :, :], both(cos_gain[:, (n % 4) // 2, :]),
                                        ALU.mult).then_inc(qk_cosined, 1)

            def qk_power(n):
                pool.wait_ge(qk_mean_done, n + 1)
                power(head_rstd[:, :], head_mean[:, :], qk_power_done)

            def out_power(p):
                pool.wait_ge(out_mean, p + 1)
                power(head_rstd[:, :], head_mean[:, :], out_power_done)

            for n in range(4):
                rotary_cos(n)
                qk_power(n)
            for n in range(4, 6):
                rotary_cos(n)
                qk_power(n)
            out_power(0)
            for n in range(6, 8):
                rotary_cos(n)
                qk_power(n)
            out_power(1)
            norm_rstd(NORM_FFN2)
            norm_rstd(NORM_FINAL)

        @block.scalar
        def _(act):
            for n in range(4):
                act.dma_start(x_res[:, 2 * n:2 * n + 2, :, :].rearrange("p s k t -> p (s k) t"),
                              x_t[:, 4 * n:4 * n + 4, :]).then_inc(x_landed[n], 16)

            def hi_parts(c, turn, slot, kn):
                act.wait_ge(landed[slot], 16 * (turn + 1))
                act.wait_ge(chunk_used, c + 1)
                half = kn * STRIP // 2
                for h in range(2):
                    nc.scalar.activation(w_split[:, slot % 2, 0, h * half:(h + 1) * half],
                                         w_raw[:, slot, h * half:(h + 1) * half], ACT.Copy).then_inc(hi_made, 1)

            def copy_lo(s, j, factor):
                act.wait_ge(chunk_used, used_value(2 * s + 1))
                act.wait_ge(psum_freed, freed_value(s - 1))
                nc.scalar.activation(lo_sum[:, j, :, :], psum[:, 2 * j:2 * j + 2, 256:512], ACT.Copy,
                                     scale=factor).then_inc(lo_copied, 1)

            def square_and_hi(q, strip, j, n, x_wait):
                act.wait_ge(*x_wait)
                act.wait_ge(params_landed, 16)
                if n != NORM_FINAL:
                    for b in range(2):
                        ins = nc.scalar.activation(x_split[:, strip, b, 0, :], x_res[:, strip, b, :], ACT.Copy,
                                                   scale=gain_by_strip[:, n, strip, b:b + 1])
                    ins.then_inc(x_hi_made, 1)
                if q >= 2:
                    act.wait_ge(squares_added, q + n)
                nc.scalar.activation(squares[:, j, :, :], x_res[:, strip, :, :], ACT.Square).then_inc(squared, 1)
                if n == NORM_FINAL:
                    act.wait_ge(squared, q + 1)
                    for b in range(2):
                        ins = nc.scalar.activation(x_res[:, strip, b, :], x_res[:, strip, b, :], ACT.Copy,
                                                   scale=gain_by_strip[:, n, strip, b:b + 1])
                    ins.then_inc(x_hi_made, 1)

            gain_by_strip = param("gain").rearrange("p (n s b) -> p n s b", n=4, b=2)

            for st in range(NS):
                square_and_hi(st, st, st % 2, 0, (x_landed[st // 2], 16))
                if st == 1:
                    hi_parts(0, 0, 0, HALF_K)
                if st == 3:
                    hi_parts(1, 0, 1, HALF_K)
            act.wait_ge(lam_ones, 1)
            nc.scalar.activation(lam_exp[:, :], psum[:, 4, 0:2], ACT.Exp).then_inc(lam_exped, 1)
            nc.scalar.activation(warm[:, :], param_sb[:, 0:1], ACT.Silu)

            def ffn_in(ph):
                def body(i):
                    s = ph["s0"] + 2 * i
                    g = ph["g0"] + i
                    turn = ph["s0"] // 2 + i
                    kn = ph["kn"]
                    hi_parts(2 * s + 2, turn, 2, kn)
                    copy_lo(s, 0, 1.0)
                    hi_parts(2 * s + 3, turn, 3, kn)
                    entry = ph["entry"] and isinstance(i, int) and i == 0

                    def silu():
                        act.wait_ge(scaled, 2 * g + 1)
                        nc.scalar.activation(silu_out[:, :, :], strip_sum[:, 0, :, :], ACT.Silu).then_inc(silu_done, 1)
                    if not entry:
                        silu()
                    kn = ph["next_kn"] if isinstance(i, int) and i == ph["bodies"] - 1 else kn
                    hi_parts(2 * s + 4, turn + 1, 0, kn)
                    if entry:
                        silu()
                    copy_lo(s + 1, 1, 1.0)
                    hi_parts(2 * s + 5, turn + 1, 1, kn)
                    act.wait_ge(hidden_done, g + 1)
                    act.wait_ge(params_landed, 16)
                    nc.scalar.activation(h_split[:, i, :, 0, :], strip_sum[:, 1, :, :], ACT.Copy).then_inc(hidden_hi, 1)
                loop(act, ph["bodies"], body, first=ph["entry"], last=ph["kn"] != ph["next_kn"])

            def residual(ph):
                n = ph["norm"]

                def norm_part(strip, j):
                    square_and_hi(8 * n + strip, strip, j, n, (res_done, ph["r0"] + strip + 1))

                def body(i):
                    at_start = isinstance(i, int) and i == 0
                    at_end = isinstance(i, int) and i == ph["bodies"] - 1
                    for j in range(2):
                        s = ph["s0"] + 2 * i + j
                        turn = ph["s0"] // 2 + i + j
                        kn = ph["next_kn"] if at_end and j else ph["kn"]
                        a, b = (2, 3) if j == 0 else (0, 1)
                        if at_start and j == 0 and ph["g0"] is None:
                            sb_hi_parts(3)
                        if kn is not None:
                            hi_parts(2 * s + 2, turn, a, kn)
                        if n is not None and not (at_start and j == 0):
                            norm_part(2 * i + j - 1, 1 - j)
                        copy_lo(s, j, ph["factor"])
                        if kn is not None:
                            hi_parts(2 * s + 3, turn, b, kn)
                        if n is not None and at_end and j:
                            norm_part(2 * i + j, j)
                if n is None:
                    loop(act, ph["bodies"], body, last=ph["kn"] != ph["next_kn"])
                else:
                    for i in range(ph["bodies"]):
                        body(i)

            def sb_hi_parts(p):
                act.wait_ge(sb_values_done, p + 1)
                nc.scalar.activation(h_split[:, 4 + p, :, 0, :], psum[:, 4:6, 0:256], ACT.Copy).then_inc(sb_hi, 1)

            def mix(ph):
                after = {cc: [] for cc in range(48)}

                def qk_square(n):
                    act.wait_ge(mix_scaled, n + 1)
                    nc.scalar.activation(squares[:, n % 2, :, :], strip_sum[:, n % 2, :, :],
                                         ACT.Square).then_inc(qk_squared, 1)

                def exps(p, maps):
                    act.wait_ge(max_step, 3 * p + 3)
                    for c in maps:
                        for b, (lo, hi) in enumerate(((0, 128), (128, 384))):
                            ins = nc.scalar.activation(prob[:, c, lo:hi], prob[:, c, lo:hi], ACT.Exp,
                                                       bias=neg_max[:, c, b:b + 1], accum_out=exp_sum[:, c, b:b + 1])
                    ins.then_inc(exped, 1)

                def exps_1(p):
                    exps(p, (0, 1))

                def exps_2(p):
                    exps(p, (2, 3))

                def turn_copy(p):
                    act.wait_ge(turned, p + 1)
                    nc.scalar.activation(prob_t[:, :, :], psum[:, 4:6, 0:384], ACT.Copy).then_inc(turn_copied, 1)

                def out_copy(p):
                    act.wait_ge(values_done, p + 1)
                    got = psum[:, 6:8, :].rearrange("p h (d t) -> p h d t", d=2)
                    nc.scalar.activation(head_out[:, :, :, :], got, ACT.Copy).then_inc(out_copied, 1)
                    nc.scalar.activation(out_sq, got, ACT.Square).then_inc(out_squared, 1)

                def out_hi_parts(p):
                    act.wait_ge(out_normed, p + 1)
                    for d in range(2):
                        ins = nc.scalar.activation(h_split[:, 2 * p:2 * p + 2, d, 0, :], head_out[:, :, d, :], ACT.Copy,
                                                   scale=subln_gain[:, d:d + 1])
                    ins.then_inc(out_hi, 1)

                def sb_logs(p):
                    act.wait_ge(sb_scores_done, p + 1)
                    got = psum[:, 4:6, 0:384]
                    nc.scalar.activation(softplus, got, ACT.Abs, scale=SCALE).then_inc(sb_abs, 1)
                    nc.scalar.activation(z, got, ACT.Copy, scale=SCALE).then_inc(sb_z, 1)
                    act.wait_ge(sb_abs, p + 1)
                    nc.scalar.activation(softplus, softplus, ACT.Exp, scale=-1.0).then_inc(sb_log, 1)
                    act.wait_ge(sb_log, 2 * p + 1)
                    nc.scalar.activation(softplus, softplus, ACT.Ln, bias=1.0).then_inc(sb_log, 1)

                def sb_exp(p):
                    act.wait_ge(sb_expo, 2 * p + 2)
                    nc.scalar.activation(sb_weight, sb_weight, ACT.Exp).then_inc(sb_weights, 1)

                for cc, kind, n in pe_steps:
                    if kind == "scores":
                        after[cc + 2].append((exps_1, n))
                        after[cc + 3].append((exps_2, n))
                    if kind == "turn":
                        after[cc].append((turn_copy, n))
                    if kind == "values":
                        after[cc].append((out_copy, n))
                    if kind == "out_spread":
                        after[cc].append((out_hi_parts, n))
                    if kind == "sb_scores":
                        after[cc].append((sb_logs, n))
                    if kind == "sb_sums":
                        after[cc].append((sb_exp, n))
                    if kind == "sb_values" and cc < 48:
                        after[cc].append((sb_hi_parts, n))
                for m, (kind, n, _) in enumerate(mix_strips):
                    s = ph["s0"] + m
                    for half in range(2):
                        cc = 2 * m + half
                        if half:
                            if kind in ("diff_qk", "sb_qk"):
                                copy_lo(s, m % 2, 1.0)
                            else:
                                act.wait_ge(chunk_used, used_value(2 * s + 1))
                                act.wait_ge(psum_freed, freed_value(s - 1))
                                act.wait_ge(norm_power, NORM_MIX + 1)
                                for b in range(2):
                                    ins = nc.scalar.activation(lo_sum[:, m % 2, b, :], psum[:, 2 * (m % 2) + b, 256:512],
                                                               ACT.Copy, scale=rstd_tok[:, b:b + 1])
                                ins.then_inc(lo_copied, 1)
                        c = 2 * ph["s0"] + cc + 2
                        hi_parts(c, c // 4, c % 4, HALF_K)
                        if half and kind == "diff_qk" and m:
                            qk_square(n)
                        if cc == 2:
                            qk_square(0)
                        for task, p in after[cc]:
                            task(p)

            for ph in phases:
                {"ffn_in": ffn_in, "residual": residual, "mix": mix}[ph["kind"]](ph)

        @block.vector
        def _(dve):
            dve.sem_inc(lo_made, LO_CREDIT)
            dve.sem_inc(psum_freed, FREED_CREDIT)
            stt = nc.vector.scalar_tensor_tensor
            gain_by_strip = param("gain").rearrange("p (n s b) -> p n s b", n=4, b=2)

            def lo_parts(c, slot, kn):
                half = kn * STRIP // 2
                for h in range(2):
                    dve.wait_ge(hi_made, hi_value(c, h))
                    part = slice(h * half, (h + 1) * half)
                    nc.vector.tensor_tensor(w_split[:, slot % 2, 1, part], w_raw[:, slot, part],
                                            w_split[:, slot % 2, 0, part].bitcast(F32), ALU.subtract).then_inc(lo_made, 1)

            def add_halves(s, j):
                dve.wait_ge(lo_copied, s + 1)
                nc.vector.tensor_tensor(strip_sum[:, j, :, :], psum[:, 2 * j:2 * j + 2, 0:256], lo_sum[:, j, :, :],
                                        ALU.add).then_inc(psum_freed, 1)
                dve.wait_ge(psum_freed, freed_value(s))

            def x_lo_and_sum(q, strip, j, n):
                if n != NORM_FINAL:
                    dve.wait_ge(x_hi_made, q + 1)
                    for b in range(2):
                        ins = stt(x_split[:, strip, b, 1, :], x_res[:, strip, b, :], gain_by_strip[:, n, strip, b:b + 1],
                                  x_split[:, strip, b, 0, :].bitcast(F32), ALU.mult, ALU.subtract)
                    ins.then_inc(x_ready, 1)
                dve.wait_ge(squared, q + 1)
                dve.wait_ge(squares_added, q + n + 1)
                nc.vector.tensor_tensor(square_sum[:, :, :], square_sum[:, :, :], squares[:, j, :, :],
                                        ALU.add).then_inc(squares_added, 1)

            def clear_sum():
                nc.vector.memset(square_sum[:, :, :], 0.0).then_inc(squares_added, 1)

            def norm_means(n):
                dve.wait_ge(norm_done, n + 1)
                nc.vector.tensor_scalar(mean_sq[:, 0:2], psum[:, 4, 0:2], 1.0 / D, EPS, ALU.mult, ALU.add).then_inc(norm_mean, 1)
                if n != NORM_FINAL:
                    clear_sum()

            def norm_diagonal(n):
                dve.wait_ge(norm_power, n + 1)
                diagonal(2, rstd_tok[:, :], norm_diag)

            def diagonal(blocks, values, done):
                nc.vector.tensor_tensor(diag[:, 0:blocks, :], const("ident").unsqueeze(1).broadcast_to([P, blocks, P]),
                                        values.unsqueeze(2).broadcast_to([P, blocks, P]), ALU.mult).then_inc(done, 1)

            def norm_copy(n):
                dve.wait_ge(norm_spread_done, n + 1)
                nc.vector.tensor_copy(rstd[:, :], psum[:, 6, 0:T]).then_inc(norm_ready, 1)
                dve.wait_ge(norm_ready, n + 1)

            clear_sum()
            dve.wait_ge(params_landed, 16)
            lam = param("lambda").rearrange("p (a b) -> p a b", b=2)
            nc.vector.tensor_tensor(lam_in[:, :], lam[:, :, 0], lam[:, :, 1], ALU.mult).then_inc(lam_ready, 1)
            nc.vector.tensor_scalar(subln_gain[:, :], param("subln"), 1.0 - LAMBDA_INIT, None, ALU.mult)
            for st in range(NS):
                x_lo_and_sum(st, st, st % 2, 0)
                if st == 1:
                    lo_parts(0, 0, HALF_K)
                if st == 3:
                    lo_parts(1, 1, HALF_K)
            dve.wait_ge(consts_landed, 16)
            for n, name in enumerate(("q_norm", "k_norm")):
                nc.vector.tensor_scalar(cos_gain[:, n, :], const("cos"), param(name), None, ALU.mult)
                nc.vector.tensor_scalar(rot_gain[0:32, n, :], const("rot")[0:32, :], param_sb[0:32, param_at[name][0]:param_at[name][1]],
                                        None, ALU.mult)
            dve.wait_ge(lam_exped, 1)
            nc.vector.tensor_tensor(lam_diff[:, :], lam_exp[:, 1:2], lam_exp[:, 0:1], ALU.subtract).then_inc(lam_ready, 1)
            dve.wait_ge(lam_ready, 2)
            nc.vector.tensor_scalar(neg_lam[:, :], lam_diff[:, :], -LAMBDA_INIT, None, ALU.add).then_inc(prepared, 1)

            def scale_strip(out, j):
                nc.vector.tensor_tensor(out, strip_sum[:, j, :, :], both(rstd[:, :]), ALU.mult).then_inc(scaled, 1)

            def ffn_in(ph):
                def body(i):
                    s = ph["s0"] + 2 * i
                    g = ph["g0"] + i
                    kn = ph["kn"]
                    entry = ph["entry"] and isinstance(i, int) and i == 0
                    lo_parts(2 * s + 2, 2, kn)
                    if entry:
                        norm_means(ph["norm"])
                    add_halves(s, 0)
                    if not entry:
                        scale_strip(strip_sum[:, 0, :, :], 0)
                    lo_parts(2 * s + 3, 3, kn)
                    if entry:
                        norm_diagonal(ph["norm"])
                    kn = ph["next_kn"] if isinstance(i, int) and i == ph["bodies"] - 1 else kn
                    lo_parts(2 * s + 4, 0, kn)
                    if entry:
                        norm_copy(ph["norm"])
                        scale_strip(strip_sum[:, 0, :, :], 0)
                    add_halves(s + 1, 1)
                    lo_parts(2 * s + 5, 1, kn)
                    scale_strip(strip_sum[:, 1, :, :], 1)
                    dve.wait_ge(silu_done, g + 1)
                    dve.wait_ge(scaled, 2 * g + 2)
                    nc.vector.tensor_tensor(strip_sum[:, 1, :, :], strip_sum[:, 1, :, :], silu_out[:, :, :],
                                            ALU.mult).then_inc(hidden_done, 1)
                    dve.wait_ge(hidden_hi, g + 1)
                    nc.vector.tensor_tensor(h_split[:, i, :, 1, :], strip_sum[:, 1, :, :],
                                            h_split[:, i, :, 0, :].bitcast(F32), ALU.subtract).then_inc(hidden_ready, 1)
                loop(dve, ph["bodies"], body, first=ph["entry"], last=ph["kn"] != ph["next_kn"])

            def residual(ph):
                n = ph["norm"]

                def body(i):
                    at_start = isinstance(i, int) and i == 0
                    at_end = isinstance(i, int) and i == ph["bodies"] - 1
                    for j in range(2):
                        s = ph["s0"] + 2 * i + j
                        strip = 2 * i + j
                        kn = ph["next_kn"] if at_end and j else ph["kn"]
                        a, b = (2, 3) if j == 0 else (0, 1)
                        if at_start and j == 0 and ph["g0"] is None:
                            sb_lo_parts(3)
                        if kn is not None:
                            lo_parts(2 * s + 2, a, kn)
                        if n is not None and not (at_start and j == 0):
                            x_lo_and_sum(8 * n + strip - 1, strip - 1, 1 - j, n)
                        dve.wait_ge(lo_copied, s + 1)
                        stt(x_res[:, strip, :, :], psum[:, 2 * j:2 * j + 2, 0:256], ph["factor"], x_res[:, strip, :, :],
                            ALU.mult, ALU.add).then_inc(psum_freed, 1)
                        if kn is not None:
                            lo_parts(2 * s + 3, b, kn)
                        dve.wait_ge(psum_freed, freed_value(s))
                        nc.vector.tensor_tensor(x_res[:, strip, :, :], x_res[:, strip, :, :], lo_sum[:, j, :, :],
                                                ALU.add).then_inc(res_done, 1)
                        if n is not None and at_end and j:
                            x_lo_and_sum(8 * n + strip, strip, j, n)
                loop(dve, ph["bodies"], body, first=n is not None, last=n is not None or ph["kn"] != ph["next_kn"])

            def sb_lo_parts(p):
                dve.wait_ge(sb_hi, p + 1)
                nc.vector.tensor_tensor(h_split[:, 4 + p, :, 1, :], psum[:, 4:6, 0:256],
                                        h_split[:, 4 + p, :, 0, :].bitcast(F32), ALU.subtract).then_inc(sb_ready, 1)

            def mix(ph):
                after = {cc: [] for cc in range(50)}

                def rotary(n):
                    dve.wait_ge(qk_normed, n + 1)
                    nc.vector.tensor_scalar(head_mean[:, :], psum[:, 4, 0:4], 1.0 / P, EPS,
                                            ALU.mult, ALU.add).then_inc(qk_mean_done, 1)
                    nc.vector.tensor_tensor(rot_sin[0:32, :, :], psum[0:32, 5, :].rearrange("p (h t) -> p h t", h=2),
                                            both(const("sin")[0:32, :]), ALU.mult).then_inc(rot_done, 1)
                    dve.wait_ge(rot_done, n + 1)
                    dve.wait_ge(qk_cosined, n + 1)
                    nc.vector.tensor_tensor(roped[0:32, :, :], roped[0:32, :, :], rot_sin[0:32, :, :],
                                            ALU.add).then_inc(qk_roped, 1)
                    dve.wait_ge(qk_power_done, n + 1)
                    diagonal(4, head_rstd[:, :], qk_diag)

                def spread_rstd():
                    return psum[:, 6, :].rearrange("p (h t) -> p h t", h=2)

                def qk_finish(n):
                    dve.wait_ge(qk_spread_done, n + 1)
                    dve.wait_ge(qk_roped, n + 1)
                    nc.vector.tensor_tensor(qk[:, n % 4, :, :], roped[:, :, :], spread_rstd(),
                                            ALU.mult).then_inc(qk_ready, 1)

                def masked(p):
                    dve.wait_ge(scores_done, p + 1)
                    mask = const("causal").unsqueeze(1).broadcast_to([P, 4, 384])
                    stt(prob[:, :, :], psum[:, 4:8, 0:384], SCALE, mask, ALU.mult, ALU.add).then_inc(scored, 1)

                def maxima(p):
                    dve.wait_ge(scored, p + 1)
                    nc.vector.tensor_reduce(seg_max[:, :, :], prob[:, :, :].rearrange("p c (g n) -> p c g n", n=P), AX_X,
                                            ALU.max).then_inc(max_step, 1)
                    dve.wait_ge(max_step, 3 * p + 1)
                    nc.vector.tensor_tensor(seg_max[:, :, 1:2], seg_max[:, :, 1:2], seg_max[:, :, 2:3],
                                            ALU.max).then_inc(max_step, 1)
                    dve.wait_ge(max_step, 3 * p + 2)
                    nc.vector.tensor_scalar(neg_max[:, :, :], seg_max[:, :, 0:2], -1.0, None, ALU.mult).then_inc(max_step, 1)

                def weights(p):
                    step = 5 * p
                    dve.wait_ge(exped, 2 * p + 2)
                    nc.vector.reciprocal(inv_sum[:, :, 0:2], exp_sum[:, :, :]).then_inc(weight_step, 1)
                    dve.wait_ge(weight_step, step + 1)
                    nc.vector.tensor_scalar(inv_sum[:, 2:4, 0:2], inv_sum[:, 2:4, 0:2], neg_lam[:, 0:1], None,
                                            ALU.mult).then_inc(weight_step, 1)
                    dve.wait_ge(weight_step, step + 2)
                    nc.vector.tensor_copy(inv_sum[:, :, 2:3], inv_sum[:, :, 1:2]).then_inc(weight_step, 1)
                    dve.wait_ge(weight_step, step + 3)
                    segs = prob[:, :, :].rearrange("p c (g n) -> p (c g) n", n=P)
                    inv = inv_sum[:, :, :].rearrange("p c g -> p (c g)").unsqueeze(2).broadcast_to([P, 12, P])
                    nc.vector.tensor_tensor(segs, segs, inv, ALU.mult).then_inc(weight_step, 1)
                    dve.wait_ge(weight_step, step + 4)
                    nc.vector.tensor_tensor(prob[:, 0:2, :], prob[:, 0:2, :], prob[:, 2:4, :], ALU.add).then_inc(weight_step, 1)

                def out_means(p):
                    dve.wait_ge(out_summed, p + 1)
                    nc.vector.tensor_scalar(head_mean[:, :], psum[:, 4, 0:4], 1.0 / (2 * P), EPS, ALU.mult,
                                            ALU.add).then_inc(out_mean, 1)
                    dve.wait_ge(out_power_done, p + 1)
                    diagonal(4, head_rstd[:, :], out_diag)

                def out_finish(p):
                    dve.wait_ge(out_spread_done, p + 1)
                    dve.wait_ge(out_copied, p + 1)
                    for h in range(2):
                        ins = nc.vector.tensor_tensor(head_out[:, h, :, :], head_out[:, h, :, :], both(psum[:, 6, h * T:(h + 1) * T]),
                                                      ALU.mult)
                    ins.then_inc(out_normed, 1)

                def out_lo_parts(p):
                    dve.wait_ge(out_hi, p + 1)
                    for d in range(2):
                        ins = stt(h_split[:, 2 * p:2 * p + 2, d, 1, :], head_out[:, :, d, :], subln_gain[:, d:d + 1],
                                  h_split[:, 2 * p:2 * p + 2, d, 0, :].bitcast(F32), ALU.mult, ALU.subtract)
                    ins.then_inc(diff_ready, 1)

                def diagonals(ap):
                    return ap.rearrange("p h (g n) -> p h g n", n=P)[:, :, 0:3:2, :]

                def on_diagonals(name):
                    return const(name).unsqueeze(1).unsqueeze(1).broadcast_to([P, 2, 2, P])

                def sb_softplus(p):
                    dve.wait_ge(sb_log, 2 * p + 2)
                    stt(softplus, z, 0.0, softplus, ALU.max, ALU.add).then_inc(sb_soft, 1)
                    dve.wait_ge(sb_soft, 2 * p + 1)
                    nc.vector.tensor_tensor(diagonals(softplus), diagonals(softplus), on_diagonals("strict"),
                                            ALU.mult).then_inc(sb_soft, 1)

                def sb_exponent(p):
                    dve.wait_ge(sb_sums_done, p + 1)
                    nc.vector.tensor_tensor(sb_weight, z, psum[:, 6:8, 0:384], ALU.subtract).then_inc(sb_expo, 1)
                    dve.wait_ge(sb_expo, 2 * p + 1)
                    nc.vector.tensor_tensor(diagonals(sb_weight), diagonals(sb_weight), on_diagonals("strict_neg"),
                                            ALU.add).then_inc(sb_expo, 1)

                for cc, kind, n in pe_steps:
                    if kind == "norm":
                        after[cc].append((norm_diagonal, n))
                    if kind == "qk_norm":
                        after[cc].append((rotary, n))
                    if kind == "qk_spread":
                        after[cc].append((qk_finish, n))
                    if kind == "scores":
                        after[cc].append((masked, n))
                        after[cc + 1].append((maxima, n))
                        after[cc + 4].append((weights, n))
                    if kind == "out_norm":
                        after[cc].append((out_means, n))
                    if kind == "out_spread":
                        after[cc].append((out_finish, n))
                        after[cc].append((out_lo_parts, n))
                    if kind == "sb_scores":
                        after[cc].append((sb_softplus, n))
                    if kind == "sb_sums":
                        after[cc].append((sb_exponent, n))
                    if kind == "sb_values" and cc < 48:
                        after[cc].append((sb_lo_parts, n))
                def mix_scale(kind, n, j):
                    out = strip_sum[:, j, :, :] if kind == "diff_qk" else qk[:, n % 2, :, :]
                    nc.vector.tensor_tensor(out, strip_sum[:, j, :, :], both(rstd[:, :]), ALU.mult).then_inc(mix_scaled, 1)

                for m, (kind, n, _) in enumerate(mix_strips):
                    s = ph["s0"] + m
                    j = m % 2
                    for half in range(2):
                        cc = 2 * m + half
                        if half:
                            if kind in ("diff_qk", "sb_qk"):
                                if m == 0:
                                    norm_means(NORM_MIX)
                                add_halves(s, j)
                                if m:
                                    mix_scale(kind, n, j)
                            else:
                                dve.wait_ge(lo_copied, s + 1)
                                for b in range(2):
                                    out = v[:, b, n % 2, :] if kind == "diff_v" else v[:, b, 0, :]
                                    ins = stt(out, psum[:, 2 * j + b, 0:256], rstd_tok[:, b:b + 1],
                                              lo_sum[:, j, b, :], ALU.mult, ALU.add)
                                    if b == 0:
                                        ins.then_inc(v_ready, 1)
                                ins.then_inc(psum_freed, 1)
                        c = 2 * ph["s0"] + cc + 2
                        lo_parts(c, c % 4, HALF_K)
                        if cc == 2:
                            norm_copy(NORM_MIX)
                            mix_scale("diff_qk", 0, 0)
                        for task, p in after[cc]:
                            task(p)

            for ph in phases:
                {"ffn_in": ffn_in, "residual": residual, "mix": mix}[ph["kind"]](ph)

            norm_means(NORM_FINAL)
            norm_diagonal(NORM_FINAL)
            norm_copy(NORM_FINAL)
            for n in range(4):
                dve.wait_ge(x_hi_made, 8 * NORM_FINAL + 2 * n + 2)
                strips = x_res[:, 2 * n:2 * n + 2, :, :].rearrange("p s b t -> p (s b) t")
                nc.vector.tensor_tensor(strips, strips, rstd[:, :].unsqueeze(1).broadcast_to([P, 4, T]),
                                        ALU.mult).then_inc(out_ready, 1)

        @block.tensor
        def _(pe):
            pe.sem_inc(chunk_used, USED_CREDIT)
            mm = nc.tensor.matmul

            def hi_lo_products(out, first, last, stationary, moving, moving_hi):
                def high():
                    return mm(out, stationary[0], moving, start=first, stop=last)

                def low():
                    return mm(out[:, 256:512], stationary[1], moving_hi, start=False, stop=False)
                if first:
                    high()
                    return low()
                low()
                return high()

            def chunk(c, slot, j, kn, second, left, block_ready=None, still=False):
                pe.wait_ge(lo_made, lo_value(c))
                w = w_split[:, slot % 2, :, 0:kn * STRIP].rearrange("p l (k n) -> p l k n", n=STRIP)
                for b in range(2):
                    cols = slice(b * P, (b + 1) * P)
                    for k in range(kn):
                        if b == 0 and block_ready is not None and block_ready(k) is not None:
                            pe.wait_ge(*block_ready(k))
                        a = left(k)
                        first = not second and k == 0
                        last = second and k == kn - 1
                        if still:
                            ins = hi_lo_products(psum[:, 2 * j + b, :], first, last,
                                                 (a[:, 0, cols], a[:, 1, cols]), w[:, :, k, :], w[:, 0, k, :])
                        else:
                            ins = hi_lo_products(psum[:, 2 * j + b, :], first, last,
                                                 (w[:, 0, k, cols], w[:, 1, k, cols]), a, a[:, 0, :])
                ins.then_inc(chunk_used, 1)

            def x_block(second):
                return lambda k: x_split[:, (HALF_K * second + k) // 2, k % 2, :, :]

            def x_strips(n, second):
                return lambda k: (x_ready, 8 * n + (HALF_K * second + k) // 2 + 1) if k % 2 == 0 else None

            def wait_banks(kind, n):
                for e in sorted(before[(kind, n)]):
                    pe.wait_ge(*bank_freed[e[0]](e[1]))

            def norm(n):
                pe.wait_ge(squares_added, 9 * n + 9)
                wait_banks("norm", n)
                for t in range(2):
                    for b in range(2):
                        ins = mm(psum[:, 4, t:t + 1], square_sum[:, b, t * P:(t + 1) * P], const("ones")[:, 0:1],
                                 start=b == 0, stop=b == 1)
                ins.then_inc(norm_done, 1)

            def spread(kind, n, blocks, ready, done):
                pe.wait_ge(ready, n + 1)
                wait_banks(kind, n)
                mm(psum[:, 6, 0:blocks * P], const("ones"), diag[:, 0:blocks, :].rearrange("p b t -> p (b t)"),
                   start=True, stop=True).then_inc(done, 1)

            def norm_spread(n):
                spread("norm_spread", n, 2, norm_diag, norm_spread_done)

            def qk_spread(n):
                spread("qk_spread", n, 4, qk_diag, qk_spread_done)

            def out_spread(p):
                spread("out_spread", p, 4, out_diag, out_spread_done)

            def ffn_in(ph):
                n = ph["norm"]

                def body(i):
                    s = ph["s0"] + 2 * i
                    pe.wait_ge(psum_freed, s + 1)
                    pe.wait_ge(x_ready, 8 * n + 4)
                    chunk(2 * s, 0, 0, ph["kn"], False, x_block(0))
                    entry = ph["entry"] and isinstance(i, int) and i == 0
                    chunk(2 * s + 1, 1, 0, ph["kn"], True, x_block(1), block_ready=x_strips(n, 1) if entry else None)
                    if entry:
                        norm(n)
                    pe.wait_ge(psum_freed, s + 2)
                    chunk(2 * s + 2, 2, 1, ph["kn"], False, x_block(0))
                    if entry:
                        norm_spread(n)
                    chunk(2 * s + 3, 3, 1, ph["kn"], True, x_block(1))
                loop(pe, ph["bodies"], body, first=ph["entry"], unroll=2)

            def residual(ph):
                kn = ph["kn"]

                def h_block(second):
                    return lambda k: h_split[:, (kn * second + k) // 2, k % 2, :, :]
                if ph["g0"] is not None:
                    ready = ((hidden_ready, ph["g0"] + kn // 2), (hidden_ready, ph["g0"] + kn))
                else:
                    ready = ((diff_ready, 2), (sb_ready, 4))

                def body(i):
                    for j in range(2):
                        s = ph["s0"] + 2 * i + j
                        pe.wait_ge(psum_freed, s + 1)
                        pe.wait_ge(*ready[0])
                        chunk(2 * s, 2 * j, j, kn, False, h_block(0))
                        if ph["g0"] is None and isinstance(i, int) and i + j == 0:
                            sb_values(3)
                        if ph["g0"] is not None:
                            pe.wait_ge(hidden_ready, ph["g0"] + kn - 1)
                        else:
                            pe.wait_ge(sb_ready, 3)
                        chunk(2 * s + 1, 2 * j + 1, j, kn, True, h_block(1),
                              block_ready=lambda k: ready[1] if k == kn - 2 else None)
                loop(pe, ph["bodies"], body, first=ph["g0"] is None, unroll=2)

            def qk_norm(n):
                pe.wait_ge(qk_squared, n + 1)
                wait_banks("qk_norm", n)
                flat = lambda ap: ap.rearrange("p h t -> p (h t)")
                for b in range(4):
                    mm(psum[:, 4, b:b + 1], squares[:, n % 2, b // 2, (b % 2) * P:(b % 2 + 1) * P], const("ones")[:, 0:1],
                       start=True, stop=True)
                mm(psum[0:32, 5, :], rot_gain[0:32, (n % 4) // 2, :], flat(strip_sum[0:32, n % 2, :, :]),
                   start=True, stop=True).then_inc(qk_normed, 1)

            def scores(p):
                pe.wait_ge(qk_ready, 4 * p + 4)
                wait_banks("scores", p)
                for c in range(4):
                    q, k = qk[:, c // 2, c % 2, :], qk[:, 2 + c // 2, c % 2, :]
                    mm(psum[:, 4 + c, 0:P], q[:, 0:P], k[:, 0:P], start=True, stop=True)
                    ins = mm(psum[:, 4 + c, P:384], q[:, P:T], k, start=True, stop=True)
                ins.then_inc(scores_done, 1)

            def turn(p):
                pe.wait_ge(weight_step, 5 * p + 5)
                wait_banks("turn", p)
                for h in range(2):
                    for b in range(3):
                        ins = nc.tensor.transpose(psum[:, 4 + h, b * P:(b + 1) * P], prob[:, h, b * P:(b + 1) * P],
                                                  const("ident"))
                ins.then_inc(turned, 1)

            def weighted_values(out, v0, v1, weights):
                mm(out, v0, weights[:, 0:T], start=True, stop=False)
                return mm(out[:, P:T], v1, weights[:, T:384], start=False, stop=True)

            def values(p):
                pe.wait_ge(turn_copied, p + 1)
                pe.wait_ge(v_ready, 2 * p + 2)
                pe.wait_ge(psum_freed, freed_value(mix_s0 + 6 * p + 5))
                wait_banks("values", p)
                for h in range(2):
                    for d in range(2):
                        cols = slice(d * P, (d + 1) * P)
                        ins = weighted_values(psum[:, 6 + h, d * T:(d + 1) * T], v[:, 0, h, cols], v[:, 1, h, cols],
                                              prob_t[:, h, :])
                ins.then_inc(values_done, 1)

            def out_norm(p):
                pe.wait_ge(out_squared, p + 1)
                wait_banks("out_norm", p)
                for b in range(4):
                    for d in range(2):
                        ins = mm(psum[:, 4, b:b + 1], out_sq[:, b // 2, d, (b % 2) * P:(b % 2 + 1) * P],
                                 const("ones")[:, 0:1], start=d == 0, stop=d == 1)
                ins.then_inc(out_summed, 1)

            def sb_scores(p):
                pe.wait_ge(mix_scaled, 8 + 2 * p + 2)
                wait_banks("sb_scores", p)
                for h in range(2):
                    q, k = qk[:, 0, h, :], qk[:, 1, h, :]
                    mm(psum[:, 4 + h, 0:T], k[:, 0:P], q, start=True, stop=True)
                    ins = mm(psum[:, 4 + h, T:384], k[:, P:T], q[:, P:T], start=True, stop=True)
                ins.then_inc(sb_scores_done, 1)

            def sb_sums(p):
                pe.wait_ge(sb_soft, 2 * p + 2)
                wait_banks("sb_sums", p)
                for h in range(2):
                    mm(psum[:, 6 + h, 0:384], const("tri"), softplus[:, h, :], start=True, stop=False)
                    ins = mm(psum[:, 6 + h, P:T], const("ones"), softplus[:, h, T:384], start=False, stop=True)
                ins.then_inc(sb_sums_done, 1)

            def sb_values(p):
                pe.wait_ge(sb_weights, p + 1)
                m = next(m for m, e in enumerate(mix_strips) if e[:2] == ("sb_v", 4 + p))
                pe.wait_ge(psum_freed, freed_value(mix_s0 + m))
                wait_banks("sb_values", p)
                for h in range(2):
                    cols = slice(h * P, (h + 1) * P)
                    ins = weighted_values(psum[:, 4 + h, 0:T], v[:, 0, 0, cols], v[:, 1, 0, cols], sb_weight[:, h, :])
                ins.then_inc(sb_values_done, 1)

            mix_s0 = next(ph["s0"] for ph in phases if ph["kind"] == "mix")
            steps = {"norm": norm, "norm_spread": norm_spread, "qk_norm": qk_norm, "qk_spread": qk_spread,
                     "out_spread": out_spread, "scores": scores, "turn": turn, "values": values,
                     "out_norm": out_norm, "sb_scores": sb_scores, "sb_sums": sb_sums, "sb_values": sb_values}

            def mix(ph):
                for m, (kind, _, _) in enumerate(mix_strips):
                    s = ph["s0"] + m
                    for half in range(2):
                        if half == 0:
                            pe.wait_ge(psum_freed, s + 1)
                        c = 2 * s + half
                        chunk(c, c % 4, m % 2, HALF_K, half == 1, x_block(half),
                              block_ready=x_strips(NORM_MIX, half) if m == 0 else None, still=kind in ("diff_v", "sb_v"))
                        for cc, step, n in pe_steps:
                            if cc == 2 * m + half:
                                steps[step](n)

            pe.wait_ge(consts_landed, 16)
            pe.wait_ge(lam_ready, 1)
            mm(psum[:, 4, 0:2], const("ones"), lam_in[:, :], start=True, stop=True).then_inc(lam_ones, 1)
            for ph in phases:
                {"ffn_in": ffn_in, "residual": residual, "mix": mix}[ph["kind"]](ph)
            norm(NORM_FINAL)
            norm_spread(NORM_FINAL)


def _constants():
    import numpy as np
    key, tok = np.arange(P), np.arange(256)
    c = {"ones": np.ones((P, P)), "ident": np.eye(P), "tri": key[:, None] >= key[None, :]}
    diag = np.where(key[:, None] >= key[None, :], 0.0, NEG)
    c["causal"] = np.concatenate([diag, np.zeros((P, P)), diag], axis=1)
    after = key[None, :] > key[:, None]
    c["strict"] = after
    c["strict_neg"] = np.where(after, 0.0, NEG)
    inv_freq = np.float32(500000.0) ** (-np.arange(0, 32, 2, dtype=np.float32) / np.float32(32))
    ang = (tok.astype(np.float32)[None, :] * inv_freq[:, None]).astype(np.float32)
    c["cos"] = np.concatenate([np.cos(ang), np.cos(ang), np.ones((P - 32, 256))], axis=0)
    c["sin"] = np.concatenate([np.sin(ang), np.sin(ang), np.zeros((P - 32, 256))], axis=0)
    rot = np.zeros((P, 32))
    for d in range(16):
        rot[d + 16, d] = -1.0
        rot[d, d + 16] = 1.0
    c["rot"] = rot
    c["minus_half"] = np.full((P, 1), -0.5)
    return np.ascontiguousarray(np.concatenate([np.asarray(c[n], np.float32) for n in CONST_COLS], axis=1))


def kernel(x, ffn1_norm, ffn1_w_gate, ffn1_w_up, ffn1_w_down, mix_norm, w_in, q_norm, k_norm, lambda_q1, lambda_k1,
           lambda_q2, lambda_k2, subln, w_out, ffn2_norm, ffn2_w_gate, ffn2_w_up, ffn2_w_down, final_norm):
    import numpy as np
    import concourse.bacc as bacc
    from concourse.bass_utils import run_bass_kernel_spmd

    _, tokens, width = x.shape
    blocks = width // P
    x_t = np.ascontiguousarray(np.asarray(x)[0].T.reshape(blocks, P, tokens).transpose(1, 0, 2))
    column = lambda a: np.asarray(a).reshape(-1, P).T
    params = np.ascontiguousarray(np.concatenate(
        [column(a) for a in (ffn1_norm, mix_norm, ffn2_norm, final_norm, q_norm, k_norm, subln,
                             lambda_q1, lambda_k1, lambda_q2, lambda_k2)], axis=1))
    arrays = {"x_t": x_t, "params": params, "consts": _constants()}
    for name, a in (("ffn1_gate", ffn1_w_gate), ("ffn1_up", ffn1_w_up), ("ffn1_down", ffn1_w_down), ("w_in", w_in),
                    ("w_out", w_out), ("ffn2_gate", ffn2_w_gate), ("ffn2_up", ffn2_w_up), ("ffn2_down", ffn2_w_down)):
        arrays[name] = np.ascontiguousarray(np.asarray(a)[0])
    nc = bacc.Bacc("TRN2", target_bir_lowering=False, num_devices=1)
    args = [nc.dram_tensor(f"in_{n}", a.shape, F32, kind="ExternalInput").ap() for n, a in arrays.items()]
    out = nc.dram_tensor("out_t", (P, blocks, tokens), F32, kind="ExternalOutput").ap()
    hybrid_layer(nc, *args, out)
    r = run_bass_kernel_spmd(nc, [{f"in_{n}": a for n, a in arrays.items()}], core_ids=[0])
    got = r.results[0]["out_t"]
    return np.ascontiguousarray(got.transpose(1, 0, 2).reshape(width, tokens).T)[None]
```

```python
from contextlib import ExitStack

import concourse.bass as bass
from concourse import mybir

F32 = mybir.dt.float32
F32R = mybir.dt.float32r
ALU = mybir.AluOpType
ACT = mybir.ActivationFunctionType
AX_X = mybir.AxisListType.X

P = 128
STRIP = 256
EPS = 1e-5
LAMBDA_INIT = 0.2
NEG = -1e30
RAW_SLOTS = 4
SPLIT_SLOTS = 2
K_SLOT = 8

CONST_COLS = {"ones": 128, "ident": 128, "minus_half": 1, "tri": 128, "causal": 384, "strict": 128,
              "strict_neg": 128, "cos": 256, "sin": 256}
FIRST_CONSTS = 257
PARAM_COLS = {"gain": 64, "q_norm": 1, "k_norm": 1, "q_swapped": 1, "k_swapped": 1, "subln": 2, "lambda": 4}
NORM_MIX, NORM_FFN2, NORM_FINAL = 1, 2, 3


def columns(table):
    at, out = 0, {}
    for name, n in table.items():
        out[name] = (at, at + n)
        at += n
    return out, at


def hybrid_layer(nc, x_t, params, consts, ffn1_gate, ffn1_up, ffn1_down, w_in, w_out,
                 ffn2_gate, ffn2_up, ffn2_down, out_t):
    D = w_out.shape[1]
    FF = ffn1_gate.shape[1]
    T = x_t.shape[2]
    KB = D // P
    NS = D // STRIP
    HALF_K = KB // 2
    assert T == 256 and KB == 16 and FF % (2 * STRIP) == 0
    SCALE = float(P) ** -0.5

    phases = []
    s = g = r = 0
    ff_parts = []
    at = 0
    for n in (8, 8, FF // STRIP - 16):
        ff_parts.append((at, n))
        at += n
    def plan_ffn(gate, up, down, norm_in, norm_out):
        nonlocal s, g, r
        for part, (f0, n) in enumerate(ff_parts):
            phases.append({"kind": "ffn_in", "s0": s, "g0": g, "bodies": n, "kn": HALF_K, "f0": f0,
                           "gate": gate, "up": up, "norm": norm_in, "entry": part == 0})
            s, g = s + 2 * n, g + n
            last = part == len(ff_parts) - 1
            phases.append({"kind": "residual", "s0": s, "r0": r, "bodies": NS // 2, "kn": n, "k0": 2 * f0,
                           "w": down, "g0": g - n, "factor": 0.5, "norm": norm_out if last else None})
            s, r = s + NS, r + NS
    plan_ffn(ffn1_gate, ffn1_up, ffn1_down, 0, NORM_MIX)
    phases.append({"kind": "mix", "s0": s, "bodies": 12, "kn": HALF_K})
    s += 24
    phases.append({"kind": "residual", "s0": s, "r0": r, "bodies": NS // 2, "kn": HALF_K, "k0": 0,
                   "w": w_out, "g0": None, "factor": 1.0, "norm": NORM_FFN2})
    s, r = s + NS, r + NS
    plan_ffn(ffn2_gate, ffn2_up, ffn2_down, NORM_FFN2, NORM_FINAL)
    for n, ph in enumerate(phases):
        ph["next_kn"] = phases[n + 1]["kn"] if n + 1 < len(phases) else None

    QK = D // 4
    SBW = D // 2
    mix_strips = []
    for p in range(2):
        for t in range(4):
            mix_strips.append(("diff_qk", 4 * p + t, (t * QK) // STRIP + p))
        for h in range(2):
            mix_strips.append(("diff_v", 2 * p + h, (4 * QK) // STRIP + 2 * p + h))
    sb0 = (4 * QK + SBW) // STRIP
    sb = lambda kind, p: (("sb_v", 4 + p, sb0 + 2 * (SBW // STRIP) + p) if kind == "v" else
                          ("sb_qk", 2 * p + (kind == "k"), sb0 + (kind == "k") * (SBW // STRIP) + p))
    for kind, p in (("q", 0), ("k", 0), ("v", 0), ("q", 1), ("k", 1), ("v", 1),
                    ("q", 2), ("k", 2), ("q", 3), ("k", 3), ("v", 2), ("v", 3)):
        mix_strips.append(sb(kind, p))

    pe_steps = [(1, "norm", NORM_MIX), (2, "norm_spread", NORM_MIX), (3, "qk_norm", 0), (4, "qk_spread", 0)]
    for n, m in enumerate((1, 2, 3, 6, 7, 8, 9), start=1):
        pe_steps += [(2 * m + 2, "qk_norm", n), (2 * m + 3, "qk_spread", n)]
    pe_steps.append((11, "lambda", 0))
    for p in range(2):
        pe_steps += [(12 * p + 10, "scores", p), (12 * p + 15, "turn", p), (12 * p + 16, "values", p),
                     (12 * p + 17, "out_norm", p), (12 * p + 18, "out_spread", p)]
    for p, (a, b, c) in enumerate(((29, 31, 33), (34, 36, 38), (40, 42, 46), (44, 46, 48))):
        pe_steps += [(a, "sb_scores", p), (b, "sb_sums", p), (c, "sb_values", p)]
    rank = {"values": 0, "sb_values": 0, "qk_spread": 0, "out_spread": 0}
    pe_steps.sort(key=lambda e: (e[0], rank.get(e[1], 1)))
    banks = {"lambda": "X", "norm": "X", "norm_spread": "Y", "qk_norm": "X", "qk_spread": "Y", "scores": "XY",
             "turn": "X", "values": "Y", "out_norm": "X", "out_spread": "Y", "sb_scores": "X", "sb_sums": "Y", "sb_values": "X"}
    order = [("norm", 0), ("norm_spread", 0)] + [e[1:] for e in pe_steps]
    order += [(kind, n) for n in (NORM_FFN2, NORM_FINAL) for kind in ("norm", "norm_spread")]
    before = {}
    for n, step in enumerate(order):
        before[step] = {next(e for e in reversed(order[:n]) if b in banks[e[0]])
                        for b in banks[step[0]] if any(b in banks[e[0]] for e in order[:n])}

    with ExitStack() as ctx:
        def sbuf(name, shape, dt=F32):
            return ctx.enter_context(nc.sbuf_tensor(name, [P, *shape], dt))

        def sem(name):
            return ctx.enter_context(nc.semaphore(name))

        x_res = sbuf("x_res", [NS, 2, T])
        x_split = sbuf("x_split", [NS, 2, 2, T], F32R)
        h_split = sbuf("h_split", [NS, 2, 2, T], F32R)
        w_raw = sbuf("w_raw", [RAW_SLOTS, K_SLOT * STRIP])
        w_split = sbuf("w_split", [SPLIT_SLOTS, 2, K_SLOT * STRIP], F32R)
        lo_sum = sbuf("lo_sum", [2, 2, T])
        strip_sum = sbuf("strip_sum", [2, 2, T])
        squares = sbuf("squares", [2, 2, T])
        silu_out = sbuf("silu_out", [2, T])
        square_sum = sbuf("square_sum", [2, T])
        mean_sq = sbuf("mean_sq", [4])
        diag = sbuf("diag", [4, P])
        rstd = sbuf("rstd", [T])
        rstd_tok = sbuf("rstd_tok", [2])
        const_at, const_n = columns(CONST_COLS)
        param_at, param_n = columns(PARAM_COLS)
        const_sb = sbuf("const_sb", [const_n])
        param_sb = sbuf("param_sb", [param_n])
        const = lambda name: const_sb[:, const_at[name][0]:const_at[name][1]]
        param = lambda name: param_sb[:, param_at[name][0]:param_at[name][1]]
        gain = param("gain").rearrange("p (n k) -> p n k", n=4)
        cos_gain = sbuf("cos_gain", [2, T])
        sin_gain = sbuf("sin_gain", [2, T])
        subln_gain = sbuf("subln_gain", [2])
        lam_in = sbuf("lam_in", [2])
        lam_exp = sbuf("lam_exp", [2])
        lam_diff = sbuf("lam_diff", [1])
        neg_lam = sbuf("neg_lam", [1])
        warm = sbuf("warm", [2])
        qk = sbuf("qk", [4, 2, T])
        v = sbuf("v", [2, 2, STRIP])
        prob = sbuf("prob", [4, 384])
        prob_t = sbuf("prob_t", [2, 384])
        head_out = sbuf("head_out", [2, 2, T])
        roped = sbuf("roped", [2, 2, T])
        partner = sbuf("partner", [2, T])
        head_mean = sbuf("head_mean", [4])
        head_rstd = sbuf("head_rstd", [4])
        seg_max = sbuf("seg_max", [4, 3])
        neg_max = sbuf("neg_max", [4, 2])
        exp_sum = sbuf("exp_sum", [4, 2])
        inv_sum = sbuf("inv_sum", [4, 2])
        out_sq = prob[:, 0:3, :].rearrange("p a b -> p (a b)")[:, 0:1024].rearrange("p (h d t) -> p h d t", h=2, d=2)
        z = prob[:, 0:2, :]
        softplus = prob[:, 2:4, :]
        sb_weight = prob_t[:, :, :]
        first_squares = [qk[:, st, :, :] for st in range(4)] + [head_out[:, h, :, :] for h in range(2)] + \
                        [squares[:, h, :, :] for h in range(2)]
        psum = ctx.enter_context(nc.psum_tensor("psum", [P, 8, 512], F32))

        DVE_OUT = ((0, 4), (4, 8), (8, 11))
        POOL_OUT = ((11, 14), (14, 16))
        x_blocks = x_res[:, :, :, :].rearrange("p s k t -> p (s k) t")

        landed = [sem(f"chunk_landed{n}") for n in range(RAW_SLOTS)]
        x_landed = [sem(f"x_landed{n}") for n in range(NS)]
        params_landed = sem("params_landed")
        norm_consts_landed = sem("norm_consts_landed")
        consts_landed = sem("consts_landed")
        quarter_landed = [[sem(f"quarter_landed{c}{q}") for q in range(3)] for c in range(2)]
        half_landed = sem("half_landed")
        even_hi = sem("even_hi")
        even_lo = sem("even_lo")
        out_written = sem("out_written")
        hi_made = sem("hi_made")
        lo_made = sem("lo_made")
        chunk_used = sem("chunk_used")
        lo_copied = sem("lo_copied")
        psum_freed = sem("psum_freed")
        scaled = sem("scaled")
        silu_done = sem("silu_done")
        hidden_done = sem("hidden_done")
        hidden_hi = sem("hidden_hi")
        hidden_ready = sem("hidden_ready")
        res_done = sem("res_done")
        first_squared = sem("first_squared")
        squared = sem("squared")
        x_hi_made = sem("x_hi_made")
        x_ready = sem("x_ready")
        squares_added = sem("squares_added")
        norm_done = sem("norm_done")
        norm_mean = sem("norm_mean")
        norm_power = sem("norm_power")
        norm_diag = sem("norm_diag")
        norm_spread_done = sem("norm_spread_done")
        norm_ready = sem("norm_ready")
        prepared = sem("prepared")
        lam_ready = sem("lam_ready")
        last_block = sem("last_block")
        last_added = sem("last_added")
        last_squared = sem("last_squared")
        out_ready = sem("out_ready")
        pool_out_ready = sem("pool_out_ready")
        lam_ones = sem("lam_ones")
        lam_exped = sem("lam_exped")
        mix_scaled = sem("mix_scaled")
        v_ready = sem("v_ready")
        qk_squared = sem("qk_squared")
        qk_cosined = sem("qk_cosined")
        qk_normed = sem("qk_normed")
        qk_mean_done = sem("qk_mean_done")
        qk_partnered = sem("qk_partnered")
        qk_sined = sem("qk_sined")
        qk_roped = sem("qk_roped")
        qk_power_done = sem("qk_power_done")
        qk_diag = sem("qk_diag")
        qk_spread_done = sem("qk_spread_done")
        qk_ready = sem("qk_ready")
        scores_done = sem("scores_done")
        scored = sem("scored")
        max_step = sem("max_step")
        exped = sem("exped")
        weight_step = sem("weight_step")
        first_map_scaled = sem("first_map_scaled")
        turned = sem("turned")
        turn_copied = sem("turn_copied")
        values_done = sem("values_done")
        out_copied = sem("out_copied")
        out_squared = sem("out_squared")
        out_summed = sem("out_summed")
        out_mean = sem("out_mean")
        out_power_done = sem("out_power_done")
        out_diag = sem("out_diag")
        out_spread_done = sem("out_spread_done")
        out_normed = sem("out_normed")
        out_hi = sem("out_hi")
        diff_ready = sem("diff_ready")
        sb_scores_done = sem("sb_scores_done")
        sb_abs = sem("sb_abs")
        sb_z = sem("sb_z")
        sb_log = sem("sb_log")
        sb_soft = sem("sb_soft")
        sb_sums_done = sem("sb_sums_done")
        sb_expo = sem("sb_expo")
        sb_weights = sem("sb_weights")
        sb_values_done = sem("sb_values_done")
        sb_hi = sem("sb_hi")
        sb_ready = sem("sb_ready")

        LAST_STRIP = phases[-1]["s0"] + NS - 1
        LO_CREDIT = 2 * RAW_SLOTS
        USED_CREDIT = SPLIT_SLOTS
        FREED_CREDIT = 2

        hi_value = lambda c, half: 2 * c + half + 1
        lo_value = lambda c: LO_CREDIT + 2 * (c + 1)
        squared_value = lambda q: q - NS + 1
        used_value = lambda c: USED_CREDIT + c + 1
        freed_value = lambda s: FREED_CREDIT + s + 1

        bank_freed = {
            "lambda": lambda n: (lam_exped, 1), "norm": lambda n: (norm_mean, n + 1),
            "norm_spread": lambda n: (norm_ready, n + 1), "qk_spread": lambda n: (qk_ready, n + 1),
            "out_spread": lambda n: (out_normed, n + 1),
            "qk_norm": lambda n: (qk_mean_done, n + 1), "scores": lambda n: (scored, n + 1),
            "turn": lambda n: (turn_copied, n + 1), "values": lambda n: (out_squared, n + 1),
            "out_norm": lambda n: (out_mean, n + 1), "sb_scores": lambda n: (sb_z, n + 1),
            "sb_sums": lambda n: (sb_expo, 2 * n + 1), "sb_values": lambda n: (sb_ready, n + 1),
        }

        def loop(eng, n, body, first=False, last=False, unroll=1):
            a, b = int(first), n - int(last)
            if first:
                body(0)
            end = a + (b - a) // unroll * unroll
            if end > a:
                with eng.Fori(a, end, unroll) as i:
                    for u in range(unroll):
                        body(i + u if u else i)
            for i in range(end, b):
                body(i)
            if last and n > int(first):
                body(n - 1)

        def both(ap):
            return ap.unsqueeze(1).broadcast_to([ap.shape[0], 2, ap.shape[1]])

        def weights_of(ph):
            def rows(w, strip, k0, kn):
                return w.rearrange("(k p) (s n) -> p k s n", p=P, n=STRIP)[:, k0:k0 + kn, strip, :]
            if ph["kind"] == "ffn_in":
                return lambda i, j: rows(ph["gate"] if j < 2 else ph["up"], ph["f0"] + i, HALF_K * (j % 2), HALF_K)
            if ph["kind"] == "residual":
                return lambda i, j: rows(ph["w"], 2 * i + j // 2, ph["k0"] + ph["kn"] * (j % 2), ph["kn"])
            return lambda i, j: rows(w_in, mix_strips[2 * i + j // 2][2], HALF_K * (j % 2), HALF_K)

        block = ctx.enter_context(nc.Block())

        @block.sync
        def _(sp):
            for ph in phases:
                source = weights_of(ph)

                def four_chunks(i):
                    for j in range(4):
                        c = 2 * ph["s0"] + 4 * i + j
                        sp.wait_ge(lo_made, 2 * c + 2)
                        dst = w_raw[:, j, 0:ph["kn"] * STRIP].rearrange("p (k n) -> p k n", n=STRIP)
                        sp.dma_start(dst, source(i, j)).then_inc(landed[j], 16)

                if ph["kind"] == "mix":
                    for i in range(ph["bodies"]):
                        four_chunks(i)
                elif ph is phases[0]:
                    def first_chunk(j, k0, kn, done):
                        dst = w_raw[:, j, k0 * STRIP:(k0 + kn) * STRIP].rearrange("p (k n) -> p k n", n=STRIP)
                        sp.dma_start(dst, source(0, j)[:, k0:k0 + kn, :]).then_inc(done, 16)
                    for st in range(NS):
                        sp.dma_start(x_res[:, st, :, :], x_t[:, 2 * st:2 * st + 2, :]).then_inc(x_landed[st], 16)
                        c, q = divmod(st, 4)
                        first_chunk(c, 2 * q, 2, landed[c] if q == 3 else quarter_landed[c][q])
                    first_chunk(2, 0, HALF_K // 2, half_landed)
                    first_chunk(2, HALF_K // 2, HALF_K // 2, landed[2])
                    sp.dma_start(const_sb[:, 0:FIRST_CONSTS], consts[:, 0:FIRST_CONSTS]).then_inc(norm_consts_landed, 16)
                    first_chunk(3, 0, HALF_K, landed[3])
                    sp.dma_start(const_sb[:, FIRST_CONSTS:], consts[:, FIRST_CONSTS:]).then_inc(consts_landed, 16)
                    with sp.Fori(1, ph["bodies"]) as i:
                        four_chunks(i)
                else:
                    loop(sp, ph["bodies"], four_chunks)
            for n, (lo, hi) in enumerate(DVE_OUT):
                sp.wait_ge(out_ready, n + 1)
                sp.dma_start(out_t[:, lo:hi, :], x_blocks[:, lo:hi, :]).then_inc(out_written, 16)
            sp.wait_ge(out_written, 16 * (len(DVE_OUT) + len(POOL_OUT)))

        @block.gpsimd
        def _(pool):
            for st in range(NS):
                pool.wait_ge(x_landed[st], 16)
                nc.gpsimd.tensor_tensor(first_squares[st], x_res[:, st, :, :], x_res[:, st, :, :],
                                        ALU.mult).then_inc(first_squared, 1)
            adds = [(st, st + 1, st + 2) for st in range(0, NS, 2)] + [(0, 2, NS + 2), (4, 6, NS + 4)]
            for a, b, needed in adds:
                pool.wait_ge(first_squared, needed)
                nc.gpsimd.tensor_tensor(first_squares[a], first_squares[a], first_squares[b], ALU.add).then_inc(first_squared, 1)
            pool.wait_ge(first_squared, NS + 6)
            nc.gpsimd.tensor_tensor(square_sum[:, :, :], first_squares[0], first_squares[4], ALU.add).then_inc(squares_added, 9)
            pool.wait_ge(norm_consts_landed, 16)

            def power(out, in_, done):
                nc.gpsimd.tensor_tensor(out, in_, const("minus_half").broadcast_to(out.shape), ALU.pow).then_inc(done, 1)

            def norm_rstd(n):
                pool.wait_ge(norm_mean, n + 1)
                power(rstd_tok[:, :], mean_sq[:, 0:2], norm_power)

            norm_rstd(0)
            norm_rstd(NORM_MIX)
            pool.wait_ge(prepared, 2)

            def rotary(n):
                pool.wait_ge(mix_scaled, n + 1)
                if n > 1:
                    pool.wait_ge(qk_ready, n - 1)
                nc.gpsimd.tensor_tensor(roped[:, n % 2, :, :], strip_sum[:, n % 2, :, :], both(cos_gain[:, (n % 4) // 2, :]),
                                        ALU.mult).then_inc(qk_cosined, 1)
                pool.wait_ge(qk_partnered, n + 1)
                nc.gpsimd.tensor_tensor(partner[0:32, :, :], partner[0:32, :, :], both(sin_gain[0:32, (n % 4) // 2, :]),
                                        ALU.mult).then_inc(qk_sined, 1)
                pool.wait_ge(qk_cosined, n + 1)
                pool.wait_ge(qk_sined, n + 1)
                nc.gpsimd.tensor_tensor(roped[0:32, n % 2, :, :], roped[0:32, n % 2, :, :], partner[0:32, :, :],
                                        ALU.add).then_inc(qk_roped, 1)

            def qk_power(n):
                pool.wait_ge(qk_mean_done, n + 1)
                power(head_rstd[:, :], head_mean[:, :], qk_power_done)

            def out_power(p):
                pool.wait_ge(out_mean, p + 1)
                power(head_rstd[:, :], head_mean[:, :], out_power_done)

            for n in range(4):
                rotary(n)
                qk_power(n)
            for n in range(4, 6):
                rotary(n)
                qk_power(n)
            out_power(0)
            for n in range(6, 8):
                rotary(n)
                qk_power(n)
            out_power(1)
            norm_rstd(NORM_FFN2)
            norm_rstd(NORM_FINAL)
            pool.wait_ge(x_hi_made, 8 * NORM_FINAL + NS)
            pool.wait_ge(norm_ready, NORM_FINAL + 1)
            for lo, hi in POOL_OUT:
                nc.gpsimd.tensor_tensor(x_blocks[:, lo:hi, :], x_blocks[:, lo:hi, :],
                                        rstd[:, :].unsqueeze(1).broadcast_to([P, hi - lo, T]), ALU.mult).then_inc(pool_out_ready, 1)

        @block.scalar
        def _(act):
            act.dma_start(param_sb[:, :], params).then_inc(params_landed, 16)
            nc.scalar.activation(warm[:, 1:2], nc.const_aps.tensor(1.0, (P, 1)), ACT.Copy)

            def hi_parts(c, turn, slot, kn):
                chunk_2 = isinstance(c, int) and c == 2
                if chunk_2:
                    act.wait_ge(half_landed, 16)
                else:
                    act.wait_ge(landed[slot], 16 * (turn + 1))
                act.wait_ge(chunk_used, c + 1)
                half = kn * STRIP // 2
                for h in range(2):
                    if chunk_2 and h:
                        act.wait_ge(landed[slot], 16)
                    nc.scalar.activation(w_split[:, slot % 2, 0, h * half:(h + 1) * half],
                                         w_raw[:, slot, h * half:(h + 1) * half], ACT.Copy).then_inc(hi_made, 1)

            def copy_lo(s, j, factor):
                act.wait_ge(chunk_used, used_value(2 * s + 1))
                act.wait_ge(psum_freed, freed_value(s - 1))
                nc.scalar.activation(lo_sum[:, j, :, :], psum[:, 2 * j:2 * j + 2, 256:512], ACT.Copy,
                                     scale=factor).then_inc(lo_copied, 1)

            def x_hi_parts(strip, n):
                for b in range(2):
                    ins = nc.scalar.activation(x_split[:, strip, b, 0, :], x_res[:, strip, b, :], ACT.Copy,
                                               scale=gain_by_strip[:, n, strip, b:b + 1])
                ins.then_inc(x_hi_made, 1)

            def square_and_hi(q, strip, j, n):
                if n != NORM_FINAL:
                    x_hi_parts(strip, n)
                if q >= 2:
                    act.wait_ge(squares_added, q + n)
                nc.scalar.activation(squares[:, j, :, :], x_res[:, strip, :, :], ACT.Square).then_inc(squared, 1)
                if n == NORM_FINAL:
                    act.wait_ge(squared, squared_value(q))
                    for b in range(2):
                        ins = nc.scalar.activation(x_res[:, strip, b, :], x_res[:, strip, b, :], ACT.Copy,
                                                   scale=gain_by_strip[:, n, strip, b:b + 1])
                    ins.then_inc(x_hi_made, 1)

            gain_by_strip = param("gain").rearrange("p (n s b) -> p n s b", n=4, b=2)

            act.wait_ge(params_landed, 16)

            for st in range(NS):
                act.wait_ge(x_landed[st], 16)
                x_hi_parts(st, 0)
                c, q = divmod(st, 4)
                act.wait_ge(landed[c] if q == 3 else quarter_landed[c][q], 16)
                cols = slice(2 * q * STRIP, 2 * (q + 1) * STRIP)
                nc.scalar.activation(w_split[:, c, 0, cols], w_raw[:, c, cols], ACT.Copy).then_inc(
                    hi_made if q % 2 else even_hi, 1)

            def ffn_in(ph):
                def body(i):
                    s = ph["s0"] + 2 * i
                    g = ph["g0"] + i
                    turn = ph["s0"] // 2 + i
                    kn = ph["kn"]
                    hi_parts(2 * s + 2, turn, 2, kn)
                    copy_lo(s, 0, 1.0)
                    hi_parts(2 * s + 3, turn, 3, kn)
                    entry = ph["entry"] and isinstance(i, int) and i == 0

                    def silu():
                        act.wait_ge(scaled, 2 * g + 1)
                        nc.scalar.activation(silu_out[:, :, :], strip_sum[:, 0, :, :], ACT.Silu).then_inc(silu_done, 1)
                    if not entry:
                        silu()
                    elif ph["norm"] == 0:
                        nc.scalar.activation(warm[:, 0:1], param_sb[:, 0:1], ACT.Silu)
                    kn = ph["next_kn"] if isinstance(i, int) and i == ph["bodies"] - 1 else kn
                    hi_parts(2 * s + 4, turn + 1, 0, kn)
                    copy_lo(s + 1, 1, 1.0)
                    hi_parts(2 * s + 5, turn + 1, 1, kn)
                    if entry:
                        silu()
                    act.wait_ge(hidden_done, g + 1)
                    act.wait_ge(params_landed, 16)
                    nc.scalar.activation(h_split[:, i, :, 0, :], strip_sum[:, 1, :, :], ACT.Copy).then_inc(hidden_hi, 1)
                loop(act, ph["bodies"], body, first=ph["entry"], last=ph["kn"] != ph["next_kn"])

            def residual(ph):
                n = ph["norm"]

                def last_strip():
                    act.wait_ge(squares_added, 8 * n + NS - 1 + n)
                    for b in range(2):
                        act.wait_ge(last_added, b + 1)
                        nc.scalar.activation(squares[:, 1, b, :], x_res[:, NS - 1, b, :], ACT.Square).then_inc(last_squared, 1)
                    act.wait_ge(last_squared, 2)
                    for b in range(2):
                        ins = nc.scalar.activation(x_res[:, NS - 1, b, :], x_res[:, NS - 1, b, :], ACT.Copy,
                                                   scale=gain_by_strip[:, n, NS - 1, b:b + 1])
                    ins.then_inc(x_hi_made, 1)

                def norm_part(strip, j):
                    act.wait_ge(res_done, ph["r0"] + strip + 1)
                    square_and_hi(8 * n + strip, strip, j, n)

                def body(i):
                    at_start = isinstance(i, int) and i == 0
                    at_end = isinstance(i, int) and i == ph["bodies"] - 1
                    for j in range(2):
                        s = ph["s0"] + 2 * i + j
                        turn = ph["s0"] // 2 + i + j
                        kn = ph["next_kn"] if at_end and j else ph["kn"]
                        a, b = (2, 3) if j == 0 else (0, 1)
                        if at_start and j == 0 and ph["g0"] is None:
                            sb_hi_parts(3)
                        if kn is not None:
                            hi_parts(2 * s + 2, turn, a, kn)
                        if n is not None and not (at_start and j == 0):
                            norm_part(2 * i + j - 1, 1 - j)
                        if n == NORM_FINAL and at_end and j:
                            last_strip()
                            continue
                        copy_lo(s, j, ph["factor"])
                        if kn is not None:
                            hi_parts(2 * s + 3, turn, b, kn)
                        if n is not None and at_end and j:
                            norm_part(2 * i + j, j)
                if n is None:
                    loop(act, ph["bodies"], body, last=ph["kn"] != ph["next_kn"])
                else:
                    for i in range(ph["bodies"]):
                        body(i)

            def sb_hi_parts(p):
                act.wait_ge(sb_values_done, p + 1)
                nc.scalar.activation(h_split[:, 4 + p, :, 0, :], psum[:, 4:6, 0:256], ACT.Copy).then_inc(sb_hi, 1)

            def mix(ph):
                after = {cc: [] for cc in range(48)}

                def qk_square(n):
                    act.wait_ge(mix_scaled, n + 1)
                    nc.scalar.activation(squares[:, n % 2, :, :], strip_sum[:, n % 2, :, :],
                                         ACT.Square).then_inc(qk_squared, 1)

                def exps(p, maps):
                    if (p, maps[0]) == (0, 0):
                        act.wait_ge(lam_ones, 1)
                        nc.scalar.activation(lam_exp[:, :], psum[:, 4, 0:2], ACT.Exp).then_inc(lam_exped, 1)
                    act.wait_ge(max_step, 3 * p + 3)
                    for c in maps:
                        for b, (lo, hi) in enumerate(((0, 128), (128, 384))):
                            ins = nc.scalar.activation(prob[:, c, lo:hi], prob[:, c, lo:hi], ACT.Exp,
                                                       bias=neg_max[:, c, b:b + 1], accum_out=exp_sum[:, c, b:b + 1])
                    ins.then_inc(exped, 1)

                def exps_1(p):
                    exps(p, (0, 1))

                def exps_2(p):
                    exps(p, (2, 3))

                def scale_first_map(p):
                    act.wait_ge(exped, 2 * p + 2)
                    act.wait_ge(weight_step, 3 * p + 1)
                    for h in range(2):
                        for b, (lo, hi) in enumerate(((0, 128), (128, 384))):
                            ins = nc.scalar.activation(prob[:, h, lo:hi], prob[:, h, lo:hi], ACT.Copy,
                                                       scale=inv_sum[:, h, b:b + 1])
                    ins.then_inc(first_map_scaled, 1)

                def turn_copy(p):
                    act.wait_ge(turned, p + 1)
                    nc.scalar.activation(prob_t[:, :, :], psum[:, 4:6, 0:384], ACT.Copy).then_inc(turn_copied, 1)

                def out_copy(p):
                    act.wait_ge(values_done, p + 1)
                    got = psum[:, 6:8, :].rearrange("p h (d t) -> p h d t", d=2)
                    nc.scalar.activation(head_out[:, :, :, :], got, ACT.Copy).then_inc(out_copied, 1)
                    nc.scalar.activation(out_sq, got, ACT.Square).then_inc(out_squared, 1)

                def out_hi_parts(p):
                    act.wait_ge(out_normed, p + 1)
                    for d in range(2):
                        ins = nc.scalar.activation(h_split[:, 2 * p:2 * p + 2, d, 0, :], head_out[:, :, d, :], ACT.Copy,
                                                   scale=subln_gain[:, d:d + 1])
                    ins.then_inc(out_hi, 1)

                def sb_logs(p):
                    act.wait_ge(sb_scores_done, p + 1)
                    got = psum[:, 4:6, 0:384]
                    nc.scalar.activation(softplus, got, ACT.Abs, scale=SCALE).then_inc(sb_abs, 1)
                    nc.scalar.activation(z, got, ACT.Copy, scale=SCALE).then_inc(sb_z, 1)
                    act.wait_ge(sb_abs, p + 1)
                    nc.scalar.activation(softplus, softplus, ACT.Exp, scale=-1.0).then_inc(sb_log, 1)
                    act.wait_ge(sb_log, 2 * p + 1)
                    nc.scalar.activation(softplus, softplus, ACT.Ln, bias=1.0).then_inc(sb_log, 1)

                def sb_exp(p):
                    act.wait_ge(sb_expo, 2 * p + 2)
                    nc.scalar.activation(sb_weight, sb_weight, ACT.Exp).then_inc(sb_weights, 1)

                for cc, kind, n in pe_steps:
                    if kind == "scores":
                        after[cc + 2].append((exps_1, n))
                        after[cc + 3].append((exps_2, n))
                        after[cc + 4].append((scale_first_map, n))
                    if kind == "turn":
                        after[cc].append((turn_copy, n))
                    if kind == "values":
                        after[cc].append((out_copy, n))
                    if kind == "out_spread":
                        after[cc + 1].append((out_hi_parts, n))
                    if kind == "sb_scores":
                        after[cc].append((sb_logs, n))
                    if kind == "sb_sums":
                        after[cc].append((sb_exp, n))
                    if kind == "sb_values" and cc < 48:
                        after[cc].append((sb_hi_parts, n))
                for m, (kind, n, _) in enumerate(mix_strips):
                    s = ph["s0"] + m
                    for half in range(2):
                        cc = 2 * m + half
                        if half:
                            if kind in ("diff_qk", "sb_qk"):
                                copy_lo(s, m % 2, 1.0)
                            else:
                                act.wait_ge(chunk_used, used_value(2 * s + 1))
                                act.wait_ge(psum_freed, freed_value(s - 1))
                                act.wait_ge(norm_power, NORM_MIX + 1)
                                for b in range(2):
                                    ins = nc.scalar.activation(lo_sum[:, m % 2, b, :], psum[:, 2 * (m % 2) + b, 256:512],
                                                               ACT.Copy, scale=rstd_tok[:, b:b + 1])
                                ins.then_inc(lo_copied, 1)
                        c = 2 * ph["s0"] + cc + 2
                        hi_parts(c, c // 4, c % 4, HALF_K)
                        if half and kind == "diff_qk" and m:
                            qk_square(n)
                        if cc == 2:
                            qk_square(0)
                        for task, p in after[cc]:
                            task(p)

            for ph in phases:
                {"ffn_in": ffn_in, "residual": residual, "mix": mix}[ph["kind"]](ph)
            for n, (lo, hi) in enumerate(POOL_OUT):
                act.wait_ge(pool_out_ready, n + 1)
                act.dma_start(out_t[:, lo:hi, :], x_blocks[:, lo:hi, :]).then_inc(out_written, 16)

        @block.vector
        def _(dve):
            dve.sem_inc(lo_made, LO_CREDIT)
            dve.sem_inc(psum_freed, FREED_CREDIT)
            stt = nc.vector.scalar_tensor_tensor
            gain_by_strip = param("gain").rearrange("p (n s b) -> p n s b", n=4, b=2)

            def lo_parts(c, slot, kn):
                half = kn * STRIP // 2
                for h in range(2):
                    dve.wait_ge(hi_made, hi_value(c, h))
                    part = slice(h * half, (h + 1) * half)
                    nc.vector.tensor_tensor(w_split[:, slot % 2, 1, part], w_raw[:, slot, part],
                                            w_split[:, slot % 2, 0, part].bitcast(F32), ALU.subtract).then_inc(lo_made, 1)

            def add_halves(s, j):
                dve.wait_ge(lo_copied, s + 1)
                nc.vector.tensor_tensor(strip_sum[:, j, :, :], psum[:, 2 * j:2 * j + 2, 0:256], lo_sum[:, j, :, :],
                                        ALU.add).then_inc(psum_freed, 1)
                dve.wait_ge(psum_freed, freed_value(s))

            def x_lo_parts(q, strip, n):
                dve.wait_ge(x_hi_made, q + 1)
                for b in range(2):
                    ins = stt(x_split[:, strip, b, 1, :], x_res[:, strip, b, :], gain_by_strip[:, n, strip, b:b + 1],
                              x_split[:, strip, b, 0, :].bitcast(F32), ALU.mult, ALU.subtract)
                ins.then_inc(x_ready, 1)

            def add_squares(q, source, n):
                dve.wait_ge(squared, squared_value(q))
                dve.wait_ge(squares_added, q + n + 1)
                nc.vector.tensor_tensor(square_sum[:, :, :], square_sum[:, :, :], source, ALU.add).then_inc(squares_added, 1)

            def x_lo_and_sum(q, strip, j, n):
                if n != NORM_FINAL:
                    x_lo_parts(q, strip, n)
                add_squares(q, squares[:, j, :, :], n)

            def clear_sum():
                nc.vector.memset(square_sum[:, :, :], 0.0).then_inc(squares_added, 1)

            def norm_means(n):
                dve.wait_ge(norm_done, n + 1)
                nc.vector.tensor_scalar(mean_sq[:, 0:2], psum[:, 4:6, 0], 1.0 / D, EPS, ALU.mult, ALU.add).then_inc(norm_mean, 1)
                if n != NORM_FINAL:
                    clear_sum()

            def norm_diagonal(n):
                if n == 0:
                    dve.wait_ge(norm_consts_landed, 16)
                dve.wait_ge(norm_power, n + 1)
                diagonal(2, rstd_tok[:, :], norm_diag)

            def diagonal(blocks, values, done):
                nc.vector.tensor_tensor(diag[:, 0:blocks, :], const("ident").unsqueeze(1).broadcast_to([P, blocks, P]),
                                        values.unsqueeze(2).broadcast_to([P, blocks, P]), ALU.mult).then_inc(done, 1)

            def norm_copy(n):
                dve.wait_ge(norm_spread_done, n + 1)
                nc.vector.tensor_copy(rstd[:, :], psum[:, 6, 0:T]).then_inc(norm_ready, 1)
                dve.wait_ge(norm_ready, n + 1)

            dve.wait_ge(params_landed, 16)
            lam = param("lambda").rearrange("p (a b) -> p a b", b=2)
            nc.vector.tensor_tensor(lam_in[:, :], lam[:, :, 0], lam[:, :, 1], ALU.mult).then_inc(lam_ready, 1)
            nc.vector.tensor_scalar(subln_gain[:, :], param("subln"), 1.0 - LAMBDA_INIT, None, ALU.mult)
            for st in range(NS):
                x_lo_parts(st, st, 0)
                c, q = divmod(st, 4)
                if q % 2:
                    dve.wait_ge(hi_made, hi_value(c, q // 2))
                else:
                    dve.wait_ge(even_hi, st // 2 + 1)
                cols = slice(2 * q * STRIP, 2 * (q + 1) * STRIP)
                nc.vector.tensor_tensor(w_split[:, c, 1, cols], w_raw[:, c, cols], w_split[:, c, 0, cols].bitcast(F32),
                                        ALU.subtract).then_inc(lo_made if q % 2 else even_lo, 1)

            def prepare():
                dve.wait_ge(consts_landed, 16)
                for n, name in enumerate(("q_norm", "k_norm")):
                    nc.vector.tensor_scalar(cos_gain[:, n, :], const("cos"), param(name), None, ALU.mult)
                    swapped = param_at[("q_swapped", "k_swapped")[n]]
                    nc.vector.tensor_scalar(sin_gain[0:32, n, :], const("sin")[0:32, :], param_sb[0:32, swapped[0]:swapped[1]],
                                            None, ALU.mult).then_inc(prepared, 1)

            def finish_lambda():
                dve.wait_ge(lam_exped, 1)
                nc.vector.tensor_tensor(lam_diff[:, :], lam_exp[:, 1:2], lam_exp[:, 0:1], ALU.subtract).then_inc(lam_ready, 1)
                dve.wait_ge(lam_ready, 2)
                nc.vector.tensor_scalar(neg_lam[:, :], lam_diff[:, :], -LAMBDA_INIT, None, ALU.add).then_inc(lam_ready, 1)
                dve.wait_ge(lam_ready, 3)

            def scale_strip(out, j):
                nc.vector.tensor_tensor(out, strip_sum[:, j, :, :], both(rstd[:, :]), ALU.mult).then_inc(scaled, 1)

            def ffn_in(ph):
                def body(i):
                    s = ph["s0"] + 2 * i
                    g = ph["g0"] + i
                    kn = ph["kn"]
                    entry = ph["entry"] and isinstance(i, int) and i == 0
                    lo_parts(2 * s + 2, 2, kn)
                    add_halves(s, 0)
                    if not entry:
                        scale_strip(strip_sum[:, 0, :, :], 0)
                    lo_parts(2 * s + 3, 3, kn)

                    def scale_silu():
                        dve.wait_ge(silu_done, g + 1)
                        nc.vector.tensor_tensor(silu_out[:, :, :], silu_out[:, :, :], both(rstd[:, :]), ALU.mult).then_inc(scaled, 1)
                    if entry:
                        norm_means(ph["norm"])
                    else:
                        scale_silu()
                    kn = ph["next_kn"] if isinstance(i, int) and i == ph["bodies"] - 1 else kn
                    lo_parts(2 * s + 4, 0, kn)
                    if entry:
                        norm_diagonal(ph["norm"])
                    add_halves(s + 1, 1)
                    if entry:
                        norm_copy(ph["norm"])
                        scale_strip(strip_sum[:, 0, :, :], 0)
                    lo_parts(2 * s + 5, 1, kn)
                    if entry:
                        scale_silu()
                    dve.wait_ge(scaled, 2 * g + 2)
                    nc.vector.tensor_tensor(strip_sum[:, 1, :, :], strip_sum[:, 1, :, :], silu_out[:, :, :],
                                            ALU.mult).then_inc(hidden_done, 1)
                    dve.wait_ge(hidden_hi, g + 1)
                    nc.vector.tensor_tensor(h_split[:, i, :, 1, :], strip_sum[:, 1, :, :],
                                            h_split[:, i, :, 0, :].bitcast(F32), ALU.subtract).then_inc(hidden_ready, 1)
                loop(dve, ph["bodies"], body, first=ph["entry"], last=ph["kn"] != ph["next_kn"])

            def residual(ph):
                n = ph["norm"]

                def body(i):
                    at_start = isinstance(i, int) and i == 0
                    at_end = isinstance(i, int) and i == ph["bodies"] - 1
                    for j in range(2):
                        s = ph["s0"] + 2 * i + j
                        strip = 2 * i + j
                        kn = ph["next_kn"] if at_end and j else ph["kn"]
                        a, b = (2, 3) if j == 0 else (0, 1)
                        if at_start and j == 0 and ph["g0"] is None:
                            sb_lo_parts(3)
                        if kn is not None:
                            lo_parts(2 * s + 2, a, kn)
                        if n is not None and not (at_start and j == 0):
                            x_lo_and_sum(8 * n + strip - 1, strip - 1, 1 - j, n)
                        if n == NORM_FINAL and at_end and j:
                            for block, done in enumerate(((last_block, 1), (chunk_used, used_value(2 * s + 1)))):
                                dve.wait_ge(*done)
                                stt(x_res[:, strip, block, :], psum[:, 2 * j + block, 0:256], ph["factor"], x_res[:, strip, block, :],
                                    ALU.mult, ALU.add).then_inc(last_added, 1)
                            continue
                        dve.wait_ge(lo_copied, s + 1)
                        stt(x_res[:, strip, :, :], psum[:, 2 * j:2 * j + 2, 0:256], ph["factor"], x_res[:, strip, :, :],
                            ALU.mult, ALU.add).then_inc(psum_freed, 1)
                        if kn is not None:
                            lo_parts(2 * s + 3, b, kn)
                        dve.wait_ge(psum_freed, freed_value(s))
                        nc.vector.tensor_tensor(x_res[:, strip, :, :], x_res[:, strip, :, :], lo_sum[:, j, :, :],
                                                ALU.add).then_inc(res_done, 1)
                        if n is not None and at_end and j:
                            x_lo_and_sum(8 * n + strip, strip, j, n)
                loop(dve, ph["bodies"], body, first=n is not None, last=n is not None or ph["kn"] != ph["next_kn"])

            def sb_lo_parts(p):
                dve.wait_ge(sb_hi, p + 1)
                nc.vector.tensor_tensor(h_split[:, 4 + p, :, 1, :], psum[:, 4:6, 0:256],
                                        h_split[:, 4 + p, :, 0, :].bitcast(F32), ALU.subtract).then_inc(sb_ready, 1)

            def mix(ph):
                after = {cc: [] for cc in range(50)}

                def partners(n):
                    dve.wait_ge(mix_scaled, n + 1)
                    if n:
                        dve.wait_ge(qk_roped, n)
                    swap = [(i + 16) % 32 for i in range(32)]
                    nc.vector.stream_shuffle(partner[0:32, :, :].rearrange("p h t -> p (h t)"),
                                             strip_sum[0:32, n % 2, :, :].rearrange("p h t -> p (h t)"),
                                             swap).then_inc(qk_partnered, 1)

                def qk_means(n):
                    dve.wait_ge(qk_normed, n + 1)
                    nc.vector.tensor_scalar(head_mean[:, :], psum[:, 4, 0:4], 1.0 / P, EPS,
                                            ALU.mult, ALU.add).then_inc(qk_mean_done, 1)

                def qk_diagonal(n):
                    dve.wait_ge(qk_power_done, n + 1)
                    diagonal(4, head_rstd[:, :], qk_diag)

                def spread_rstd():
                    return psum[:, 6, :].rearrange("p (h t) -> p h t", h=2)

                def qk_finish(n):
                    dve.wait_ge(qk_spread_done, n + 1)
                    dve.wait_ge(qk_roped, n + 1)
                    nc.vector.tensor_tensor(qk[:, n % 4, :, :], roped[:, n % 2, :, :], spread_rstd(),
                                            ALU.mult).then_inc(qk_ready, 1)

                def masked(p):
                    dve.wait_ge(scores_done, p + 1)
                    mask = const("causal").unsqueeze(1).broadcast_to([P, 4, 384])
                    stt(prob[:, :, :], psum[:, 4:8, 0:384], SCALE, mask, ALU.mult, ALU.add).then_inc(scored, 1)

                def maxima(p):
                    dve.wait_ge(scored, p + 1)
                    nc.vector.tensor_reduce(seg_max[:, :, :], prob[:, :, :].rearrange("p c (g n) -> p c g n", n=P), AX_X,
                                            ALU.max).then_inc(max_step, 1)
                    dve.wait_ge(max_step, 3 * p + 1)
                    nc.vector.tensor_tensor(seg_max[:, :, 1:2], seg_max[:, :, 1:2], seg_max[:, :, 2:3],
                                            ALU.max).then_inc(max_step, 1)
                    dve.wait_ge(max_step, 3 * p + 2)
                    nc.vector.tensor_scalar(neg_max[:, :, :], seg_max[:, :, 0:2], -1.0, None, ALU.mult).then_inc(max_step, 1)

                def inverses(p):
                    step = 3 * p
                    if p == 0:
                        finish_lambda()
                    dve.wait_ge(exped, 2 * p + 2)
                    nc.vector.reciprocal(inv_sum[:, :, :], exp_sum[:, :, :]).then_inc(weight_step, 1)
                    dve.wait_ge(weight_step, step + 1)
                    nc.vector.tensor_scalar(inv_sum[:, 2:4, :], inv_sum[:, 2:4, :], neg_lam[:, 0:1], None,
                                            ALU.mult).then_inc(weight_step, 1)

                def weights(p):
                    dve.wait_ge(weight_step, 3 * p + 2)
                    dve.wait_ge(first_map_scaled, p + 1)
                    for h in range(2):
                        for b, (lo, hi) in enumerate(((0, 128), (128, 384))):
                            ins = stt(prob[:, h, lo:hi], prob[:, 2 + h, lo:hi], inv_sum[:, 2 + h, b:b + 1],
                                      prob[:, h, lo:hi], ALU.mult, ALU.add)
                    ins.then_inc(weight_step, 1)

                def out_means(p):
                    dve.wait_ge(out_summed, p + 1)
                    nc.vector.tensor_scalar(head_mean[:, :], psum[:, 4, 0:4], 1.0 / (2 * P), EPS, ALU.mult,
                                            ALU.add).then_inc(out_mean, 1)

                def out_diagonal(p):
                    dve.wait_ge(out_power_done, p + 1)
                    diagonal(4, head_rstd[:, :], out_diag)

                def out_finish(p):
                    dve.wait_ge(out_spread_done, p + 1)
                    dve.wait_ge(out_copied, p + 1)
                    for h in range(2):
                        ins = nc.vector.tensor_tensor(head_out[:, h, :, :], head_out[:, h, :, :], both(psum[:, 6, h * T:(h + 1) * T]),
                                                      ALU.mult)
                    ins.then_inc(out_normed, 1)

                def out_lo_parts(p):
                    dve.wait_ge(out_hi, p + 1)
                    for d in range(2):
                        ins = stt(h_split[:, 2 * p:2 * p + 2, d, 1, :], head_out[:, :, d, :], subln_gain[:, d:d + 1],
                                  h_split[:, 2 * p:2 * p + 2, d, 0, :].bitcast(F32), ALU.mult, ALU.subtract)
                    ins.then_inc(diff_ready, 1)

                def diagonals(ap):
                    return ap.rearrange("p h (g n) -> p h g n", n=P)[:, :, 0:3:2, :]

                def on_diagonals(name):
                    return const(name).unsqueeze(1).unsqueeze(1).broadcast_to([P, 2, 2, P])

                def sb_softplus(p):
                    dve.wait_ge(sb_log, 2 * p + 2)
                    stt(softplus, z, 0.0, softplus, ALU.max, ALU.add).then_inc(sb_soft, 1)
                    dve.wait_ge(sb_soft, 2 * p + 1)
                    nc.vector.tensor_tensor(diagonals(softplus), diagonals(softplus), on_diagonals("strict"),
                                            ALU.mult).then_inc(sb_soft, 1)

                def sb_exponent(p):
                    dve.wait_ge(sb_sums_done, p + 1)
                    nc.vector.tensor_tensor(sb_weight, z, psum[:, 6:8, 0:384], ALU.subtract).then_inc(sb_expo, 1)
                    dve.wait_ge(sb_expo, 2 * p + 1)
                    nc.vector.tensor_tensor(diagonals(sb_weight), diagonals(sb_weight), on_diagonals("strict_neg"),
                                            ALU.add).then_inc(sb_expo, 1)

                early = {cc: [] for cc in range(50)}
                for cc, kind, n in sorted(pe_steps, key=lambda e: (e[0], e[1] != "out_spread", e[1] != "qk_norm")):
                    if kind == "norm":
                        early[cc].append((norm_means, n))
                        after[cc].append((norm_diagonal, n))
                    if kind == "qk_norm":
                        early[cc].append((qk_means, n))
                        after[cc].append((qk_diagonal, n))
                        after[cc - 1].insert(0, (partners, n))
                    if kind == "qk_spread":
                        after[cc].append((qk_finish, n))
                    if kind == "out_norm":
                        early[cc].append((out_means, n))
                        after[cc].append((out_diagonal, n))
                    if kind == "out_spread":
                        after[cc].append((out_finish, n))
                        after[cc + 2].append((out_lo_parts, n))
                    if kind == "sb_scores":
                        after[cc].append((sb_softplus, n))
                    if kind == "sb_sums":
                        after[cc].append((sb_exponent, n))
                    if kind == "sb_values" and cc < 48:
                        after[cc].append((sb_lo_parts, n))
                for cc, kind, n in pe_steps:
                    if kind == "scores":
                        after[cc].append((masked, n))
                        after[cc + 1].append((maxima, n))
                        after[cc + 3].append((inverses, n))
                        after[cc + 4].append((weights, n))
                def mix_scale(kind, n, j):
                    out = strip_sum[:, j, :, :] if kind == "diff_qk" else qk[:, n % 2, :, :]
                    nc.vector.tensor_tensor(out, strip_sum[:, j, :, :], both(rstd[:, :]), ALU.mult).then_inc(mix_scaled, 1)

                for m, (kind, n, _) in enumerate(mix_strips):
                    s = ph["s0"] + m
                    j = m % 2
                    for half in range(2):
                        cc = 2 * m + half
                        if half:
                            if kind in ("diff_qk", "sb_qk"):
                                add_halves(s, j)
                                if m:
                                    mix_scale(kind, n, j)
                            else:
                                dve.wait_ge(lo_copied, s + 1)
                                for b in range(2):
                                    out = v[:, b, n % 2, :] if kind == "diff_v" else v[:, b, 0, :]
                                    ins = stt(out, psum[:, 2 * j + b, 0:256], rstd_tok[:, b:b + 1],
                                              lo_sum[:, j, b, :], ALU.mult, ALU.add)
                                    if b == 0:
                                        ins.then_inc(v_ready, 1)
                                ins.then_inc(psum_freed, 1)
                        c = 2 * ph["s0"] + cc + 2
                        for task, p in early[cc]:
                            task(p)
                        lo_parts(c, c % 4, HALF_K)
                        if cc == 2:
                            norm_copy(NORM_MIX)
                            mix_scale("diff_qk", 0, 0)
                        for task, p in after[cc]:
                            task(p)

            for ph in phases:
                {"ffn_in": ffn_in, "residual": residual, "mix": mix}[ph["kind"]](ph)
                if ph is phases[1]:
                    prepare()

            norm_means(NORM_FINAL)
            norm_diagonal(NORM_FINAL)
            norm_copy(NORM_FINAL)
            dve.wait_ge(x_hi_made, 8 * NORM_FINAL + NS)
            for lo, hi in DVE_OUT:
                nc.vector.tensor_tensor(x_blocks[:, lo:hi, :], x_blocks[:, lo:hi, :],
                                        rstd[:, :].unsqueeze(1).broadcast_to([P, hi - lo, T]), ALU.mult).then_inc(out_ready, 1)

        @block.tensor
        def _(pe):
            pe.sem_inc(chunk_used, USED_CREDIT)
            mm = nc.tensor.matmul

            def hi_lo_products(out, first, last, stationary, moving, moving_hi, merged):
                def high():
                    return mm(out, stationary[0], moving, start=first, stop=last)

                def low():
                    return mm(out[:, 256:512], stationary[1], moving_hi, start=False, stop=False)
                if merged:
                    moving_lo = moving[:, 1, :]
                    mm(out[:, 0:256], stationary[0], moving_hi, start=first, stop=False)
                    mm(out[:, 0:256], stationary[1], moving_hi, start=False, stop=False)
                    return mm(out[:, 0:256], stationary[0], moving_lo, start=False, stop=last)
                if first:
                    high()
                    return low()
                low()
                return high()

            def chunk(c, slot, j, kn, second, left, block_ready=None, still=False, first_two=False, merged=False,
                      block_done=None):
                if not first_two:
                    pe.wait_ge(lo_made, lo_value(c))
                w = w_split[:, slot % 2, :, 0:kn * STRIP].rearrange("p l (k n) -> p l k n", n=STRIP)
                for b, k in [(b, k) for k in range(kn) for b in range(2)] if first_two else \
                        [(b, k) for b in range(2) for k in range(kn)]:
                    cols = slice(b * P, (b + 1) * P)
                    if first_two and b == 0 and k % 4 == 0:
                        pe.wait_ge(even_lo, 2 * c + k // 4 + 1)
                    if first_two and b == 0 and k % 4 == 2:
                        pe.wait_ge(lo_made, lo_value(c) - (k == 2))
                    if b == 0 and block_ready is not None and block_ready(k) is not None:
                        pe.wait_ge(*block_ready(k))
                    a = left(k)
                    first = not second and k == 0
                    last = second and k == kn - 1
                    if still:
                        ins = hi_lo_products(psum[:, 2 * j + b, :], first, last,
                                             (a[:, 0, cols], a[:, 1, cols]), w[:, :, k, :], w[:, 0, k, :], False)
                    else:
                        ins = hi_lo_products(psum[:, 2 * j + b, :], first, last,
                                             (w[:, 0, k, cols], w[:, 1, k, cols]), a, a[:, 0, :], merged)
                    if block_done is not None and (b, k) == (0, kn - 1):
                        ins.then_inc(block_done, 1)
                ins.then_inc(chunk_used, 1)

            def x_block(second):
                return lambda k: x_split[:, (HALF_K * second + k) // 2, k % 2, :, :]

            def x_strips(n, second):
                return lambda k: (x_ready, 8 * n + (HALF_K * second + k) // 2 + 1) if k % 2 == 0 else None

            def wait_banks(kind, n):
                for e in sorted(before[(kind, n)]):
                    pe.wait_ge(*bank_freed[e[0]](e[1]))

            def norm(n):
                if n == 0:
                    pe.wait_ge(norm_consts_landed, 16)
                pe.wait_ge(squares_added, 9 * n + (8 if n == NORM_FINAL else 9))
                wait_banks("norm", n)

                def add(sq, t, start, stop):
                    return mm(psum[:, 4 + t, 0:1], sq[:, t * P:(t + 1) * P], const("ones")[:, 0:1], start=start, stop=stop)
                for t in range(2):
                    for b in range(2):
                        ins = add(square_sum[:, b, :], t, b == 0, n != NORM_FINAL and b == 1)
                if n == NORM_FINAL:
                    for b in range(2):
                        pe.wait_ge(last_squared, b + 1)
                        for t in range(2):
                            ins = add(squares[:, 1, b, :], t, False, b == 1)
                ins.then_inc(norm_done, 1)

            def spread(kind, n, blocks, ready, done):
                pe.wait_ge(ready, n + 1)
                wait_banks(kind, n)
                mm(psum[:, 6, 0:blocks * P], const("ones"), diag[:, 0:blocks, :].rearrange("p b t -> p (b t)"),
                   start=True, stop=True).then_inc(done, 1)

            def norm_spread(n):
                spread("norm_spread", n, 2, norm_diag, norm_spread_done)

            def qk_spread(n):
                spread("qk_spread", n, 4, qk_diag, qk_spread_done)

            def out_spread(p):
                spread("out_spread", p, 4, out_diag, out_spread_done)

            def ffn_in(ph):
                n = ph["norm"]

                def body(i):
                    s = ph["s0"] + 2 * i
                    pe.wait_ge(psum_freed, s + 1)
                    entry = ph["entry"] and isinstance(i, int) and i == 0
                    ready = [x_strips(n, half) if entry else None for half in range(2)]
                    start = entry and n == 0
                    chunk(2 * s, 0, 0, ph["kn"], False, x_block(0), block_ready=ready[0], first_two=start)
                    chunk(2 * s + 1, 1, 0, ph["kn"], True, x_block(1), block_ready=ready[1], first_two=start)
                    pe.wait_ge(psum_freed, s + 2)
                    chunk(2 * s + 2, 2, 1, ph["kn"], False, x_block(0))
                    if entry:
                        norm(n)
                    chunk(2 * s + 3, 3, 1, ph["kn"], True, x_block(1))
                    if entry:
                        norm_spread(n)
                loop(pe, ph["bodies"], body, first=ph["entry"], unroll=2)

            def residual(ph):
                kn = ph["kn"]

                def h_block(second):
                    return lambda k: h_split[:, (kn * second + k) // 2, k % 2, :, :]
                if ph["g0"] is not None:
                    ready = ((hidden_ready, ph["g0"] + kn // 2), (hidden_ready, ph["g0"] + kn))
                else:
                    ready = ((diff_ready, 2), (sb_ready, 4))

                def body(i):
                    for j in range(2):
                        s = ph["s0"] + 2 * i + j
                        very_last = isinstance(s, int) and s == LAST_STRIP
                        pe.wait_ge(psum_freed, s + 1)
                        pe.wait_ge(*ready[0])
                        chunk(2 * s, 2 * j, j, kn, False, h_block(0), merged=very_last)
                        if ph["g0"] is None and isinstance(i, int) and i + j == 0:
                            sb_values(3)
                        if ph["g0"] is not None:
                            pe.wait_ge(hidden_ready, ph["g0"] + kn - 1)
                        else:
                            pe.wait_ge(sb_ready, 3)
                        chunk(2 * s + 1, 2 * j + 1, j, kn, True, h_block(1),
                              block_ready=lambda k: ready[1] if k == kn - 2 else None,
                              merged=very_last, block_done=last_block if very_last else None)
                loop(pe, ph["bodies"], body, first=ph["g0"] is None, last=ph["norm"] == NORM_FINAL, unroll=2)

            def qk_norm(n):
                pe.wait_ge(qk_squared, n + 1)
                wait_banks("qk_norm", n)
                for b in range(4):
                    ins = mm(psum[:, 4, b:b + 1], squares[:, n % 2, b // 2, (b % 2) * P:(b % 2 + 1) * P],
                             const("ones")[:, 0:1], start=True, stop=True)
                ins.then_inc(qk_normed, 1)

            def scores(p):
                pe.wait_ge(qk_ready, 4 * p + 4)
                wait_banks("scores", p)
                for c in range(4):
                    q, k = qk[:, c // 2, c % 2, :], qk[:, 2 + c // 2, c % 2, :]
                    mm(psum[:, 4 + c, 0:P], q[:, 0:P], k[:, 0:P], start=True, stop=True)
                    ins = mm(psum[:, 4 + c, P:384], q[:, P:T], k, start=True, stop=True)
                ins.then_inc(scores_done, 1)

            def turn(p):
                pe.wait_ge(weight_step, 3 * p + 3)
                wait_banks("turn", p)
                for h in range(2):
                    for b in range(3):
                        ins = nc.tensor.transpose(psum[:, 4 + h, b * P:(b + 1) * P], prob[:, h, b * P:(b + 1) * P],
                                                  const("ident"))
                ins.then_inc(turned, 1)

            def weighted_values(out, v0, v1, weights):
                mm(out, v0, weights[:, 0:T], start=True, stop=False)
                return mm(out[:, P:T], v1, weights[:, T:384], start=False, stop=True)

            def values(p):
                pe.wait_ge(turn_copied, p + 1)
                pe.wait_ge(v_ready, 2 * p + 2)
                pe.wait_ge(psum_freed, freed_value(mix_s0 + 6 * p + 5))
                wait_banks("values", p)
                for h in range(2):
                    for d in range(2):
                        cols = slice(d * P, (d + 1) * P)
                        ins = weighted_values(psum[:, 6 + h, d * T:(d + 1) * T], v[:, 0, h, cols], v[:, 1, h, cols],
                                              prob_t[:, h, :])
                ins.then_inc(values_done, 1)

            def out_norm(p):
                pe.wait_ge(out_squared, p + 1)
                wait_banks("out_norm", p)
                for b in range(4):
                    for d in range(2):
                        ins = mm(psum[:, 4, b:b + 1], out_sq[:, b // 2, d, (b % 2) * P:(b % 2 + 1) * P],
                                 const("ones")[:, 0:1], start=d == 0, stop=d == 1)
                ins.then_inc(out_summed, 1)

            def sb_scores(p):
                pe.wait_ge(mix_scaled, 8 + 2 * p + 2)
                wait_banks("sb_scores", p)
                for h in range(2):
                    q, k = qk[:, 0, h, :], qk[:, 1, h, :]
                    mm(psum[:, 4 + h, 0:T], k[:, 0:P], q, start=True, stop=True)
                    ins = mm(psum[:, 4 + h, T:384], k[:, P:T], q[:, P:T], start=True, stop=True)
                ins.then_inc(sb_scores_done, 1)

            def sb_sums(p):
                pe.wait_ge(sb_soft, 2 * p + 2)
                wait_banks("sb_sums", p)
                for h in range(2):
                    mm(psum[:, 6 + h, 0:384], const("tri"), softplus[:, h, :], start=True, stop=False)
                    ins = mm(psum[:, 6 + h, P:T], const("ones"), softplus[:, h, T:384], start=False, stop=True)
                ins.then_inc(sb_sums_done, 1)

            def sb_values(p):
                pe.wait_ge(sb_weights, p + 1)
                m = next(m for m, e in enumerate(mix_strips) if e[:2] == ("sb_v", 4 + p))
                pe.wait_ge(psum_freed, freed_value(mix_s0 + m))
                wait_banks("sb_values", p)
                for h in range(2):
                    cols = slice(h * P, (h + 1) * P)
                    ins = weighted_values(psum[:, 4 + h, 0:T], v[:, 0, 0, cols], v[:, 1, 0, cols], sb_weight[:, h, :])
                ins.then_inc(sb_values_done, 1)

            def lambda_sums(_):
                pe.wait_ge(lam_ready, 1)
                wait_banks("lambda", 0)
                mm(psum[:, 4, 0:2], const("ones"), lam_in[:, :], start=True, stop=True).then_inc(lam_ones, 1)

            mix_s0 = next(ph["s0"] for ph in phases if ph["kind"] == "mix")
            steps = {"lambda": lambda_sums, "norm": norm, "norm_spread": norm_spread, "qk_norm": qk_norm, "qk_spread": qk_spread,
                     "out_spread": out_spread, "scores": scores, "turn": turn, "values": values,
                     "out_norm": out_norm, "sb_scores": sb_scores, "sb_sums": sb_sums, "sb_values": sb_values}

            def mix(ph):
                for m, (kind, _, _) in enumerate(mix_strips):
                    s = ph["s0"] + m
                    for half in range(2):
                        if half == 0:
                            pe.wait_ge(psum_freed, s + 1)
                        c = 2 * s + half
                        chunk(c, c % 4, m % 2, HALF_K, half == 1, x_block(half),
                              block_ready=x_strips(NORM_MIX, half) if m == 0 else None, still=kind in ("diff_v", "sb_v"))
                        for cc, step, n in pe_steps:
                            if cc == 2 * m + half:
                                steps[step](n)

            for ph in phases:
                {"ffn_in": ffn_in, "residual": residual, "mix": mix}[ph["kind"]](ph)
                if ph is phases[1]:
                    pe.wait_ge(consts_landed, 16)
            norm(NORM_FINAL)
            norm_spread(NORM_FINAL)


def _constants():
    import numpy as np
    key, tok = np.arange(P), np.arange(256)
    c = {"ones": np.ones((P, P)), "ident": np.eye(P), "tri": key[:, None] >= key[None, :]}
    diag = np.where(key[:, None] >= key[None, :], 0.0, NEG)
    c["causal"] = np.concatenate([diag, np.zeros((P, P)), diag], axis=1)
    after = key[None, :] > key[:, None]
    c["strict"] = after
    c["strict_neg"] = np.where(after, 0.0, NEG)
    inv_freq = np.float32(500000.0) ** (-np.arange(0, 32, 2, dtype=np.float32) / np.float32(32))
    ang = (tok.astype(np.float32)[None, :] * inv_freq[:, None]).astype(np.float32)
    c["cos"] = np.concatenate([np.cos(ang), np.cos(ang), np.ones((P - 32, 256))], axis=0)
    c["sin"] = np.concatenate([-np.sin(ang), np.sin(ang), np.zeros((P - 32, 256))], axis=0)
    c["minus_half"] = np.full((P, 1), -0.5)
    return np.ascontiguousarray(np.concatenate([np.asarray(c[n], np.float32) for n in CONST_COLS], axis=1))


def kernel(x, ffn1_norm, ffn1_w_gate, ffn1_w_up, ffn1_w_down, mix_norm, w_in, q_norm, k_norm, lambda_q1, lambda_k1,
           lambda_q2, lambda_k2, subln, w_out, ffn2_norm, ffn2_w_gate, ffn2_w_up, ffn2_w_down, final_norm):
    import numpy as np
    import concourse.bacc as bacc
    from concourse.bass_utils import run_bass_kernel_spmd

    _, tokens, width = x.shape
    blocks = width // P
    x_t = np.ascontiguousarray(np.asarray(x)[0].T.reshape(blocks, P, tokens).transpose(1, 0, 2))
    column = lambda a: np.asarray(a).reshape(-1, P).T
    swapped = lambda a: np.concatenate([np.asarray(a)[..., 16:32], np.asarray(a)[..., 0:16], np.asarray(a)[..., 32:]], axis=-1)
    params = np.ascontiguousarray(np.concatenate(
        [column(a) for a in (ffn1_norm, mix_norm, ffn2_norm, final_norm, q_norm, k_norm, swapped(q_norm), swapped(k_norm), subln,
                             lambda_q1, lambda_k1, lambda_q2, lambda_k2)], axis=1))
    arrays = {"x_t": x_t, "params": params, "consts": _constants()}
    for name, a in (("ffn1_gate", ffn1_w_gate), ("ffn1_up", ffn1_w_up), ("ffn1_down", ffn1_w_down), ("w_in", w_in),
                    ("w_out", w_out), ("ffn2_gate", ffn2_w_gate), ("ffn2_up", ffn2_w_up), ("ffn2_down", ffn2_w_down)):
        arrays[name] = np.ascontiguousarray(np.asarray(a)[0])
    nc = bacc.Bacc("TRN2", target_bir_lowering=False, num_devices=1)
    args = [nc.dram_tensor(f"in_{n}", a.shape, F32, kind="ExternalInput").ap() for n, a in arrays.items()]
    out = nc.dram_tensor("out_t", (P, blocks, tokens), F32, kind="ExternalOutput").ap()
    hybrid_layer(nc, *args, out)
    r = run_bass_kernel_spmd(nc, [{f"in_{n}": a for n, a in arrays.items()}], core_ids=[0])
    got = r.results[0]["out_t"]
    return np.ascontiguousarray(got.transpose(1, 0, 2).reshape(width, tokens).T)[None]
```
